# Optimizing a Trainium2 kernel written in Bass

```python
import jax, jax.numpy as jnp
from jax import lax
import numpy as np

D_MODEL = 2048
BATCH = 1
SEQ = 256
DEPTH = 1
DEC_BATCH = 8
DEC_SEQ = 4
PAST_LEN = 2048
PAGE_SIZE = 128

RWKV_WIDTH = D_MODEL // 2
RWKV_HEAD = 64
RWKV_HEADS = RWKV_WIDTH // RWKV_HEAD
DECAY_LORA = 96
AAA_LORA = 96
GATE_LORA = 256
MLA_V = 128
MLA_HEADS = (D_MODEL - RWKV_WIDTH) // MLA_V
MLA_WIDTH = MLA_HEADS * MLA_V
MLA_NOPE = 128
MLA_ROPE = 64
Q_RANK = 512
KV_RANK = 256
D_FF = 4 * D_MODEL
ROPE_THETA = 10000.0
Q_BLOCK = 128
N_SHIFT = 3 * RWKV_WIDTH + DECAY_LORA + AAA_LORA + GATE_LORA
N_IN = N_SHIFT + Q_RANK + KV_RANK + MLA_ROPE
DEEPNORM_ALPHA = (2.0 * DEPTH) ** 0.25
DEEPNORM_BETA = (8.0 * DEPTH) ** -0.25
LN_EPS = 1e-5
RMS_EPS = 1e-6
GN_EPS = 64e-5

kernel_name = "hymba_rwkv7_mla_deepnorm_adaln_step"

F32 = jnp.float32

def _layernorm(x, g, b):
    xf = x.astype(F32)
    mu = jnp.mean(xf, -1, keepdims=True)
    var = jnp.mean(jnp.square(xf - mu), -1, keepdims=True)
    return ((xf - mu) * lax.rsqrt(var + LN_EPS) * g + b).astype(x.dtype)

def _rmsnorm(x, g):
    xf = x.astype(F32)
    return (xf * lax.rsqrt(jnp.mean(xf * xf, -1, keepdims=True) + RMS_EPS) * g).astype(x.dtype)

def _rope(x, pos):
    half = MLA_ROPE // 2
    inv = ROPE_THETA ** (-jnp.arange(half, dtype=F32) / half)
    ang = pos.astype(F32)[:, None] * inv
    ang = ang.reshape(ang.shape[:1] + (1,) * (x.ndim - 3) + (half,))
    cos, sin = jnp.cos(ang), jnp.sin(ang)
    xf = x.astype(F32)
    x1, x2 = xf[..., :half], xf[..., half:]
    return jnp.concatenate([x1 * cos - x2 * sin, x1 * sin + x2 * cos], -1).astype(x.dtype)

def _latent_attend(q_lat, q_rope, lat, kr, q_pos, k_pos):
    scale = (MLA_NOPE + MLA_ROPE) ** -0.5
    latf = lat.astype(F32)
    s = (jnp.einsum('qhr,kr->hqk', q_lat.astype(F32), latf)
         + jnp.einsum('qhd,kd->hqk', q_rope.astype(F32), kr.astype(F32))) * scale
    s = jnp.where(k_pos[None, None, :] <= q_pos[None, :, None], s, -jnp.inf)
    p = jax.nn.softmax(s, axis=-1)
    return jnp.einsum('hqk,kr->qhr', p, latf)

def _prompt_attention(q_lat, q_rope, lat, kr):
    B, T = q_lat.shape[:2]
    nb = T // Q_BLOCK
    pos = jnp.arange(T)

    def blk(args):
        ql, qr, qp = args
        return jax.vmap(_latent_attend, in_axes=(0, 0, 0, 0, None, None))(ql, qr, lat, kr, qp, pos)

    split = lambda a: a.reshape((B, nb, Q_BLOCK) + a.shape[2:]).swapaxes(0, 1)
    out = lax.map(blk, (split(q_lat), split(q_rope), pos.reshape(nb, Q_BLOCK)))
    return out.swapaxes(0, 1).reshape((B, T) + out.shape[3:])

def _sample_attention(q_lat, q_rope, lat, kr, cache_lat, cache_kr, page_table):
    T = q_lat.shape[1]
    past = page_table.shape[1] * cache_lat.shape[1]
    q_pos = past + jnp.arange(T)
    k_pos = jnp.arange(past + T)

    def one(args):
        ql, qr, ln, kn, pt = args
        lat_all = jnp.concatenate([cache_lat[pt].reshape(past, -1), ln.astype(cache_lat.dtype)], 0)
        kr_all = jnp.concatenate([cache_kr[pt].reshape(past, -1), kn.astype(cache_kr.dtype)], 0)
        return _latent_attend(ql, qr, lat_all, kr_all, q_pos, k_pos)

    return lax.map(one, (q_lat, q_rope, lat, kr, page_table))

def _wkv_scan(S0, r, decay, k, v, kk, a):
    def step(S, inp):
        r_t, w_t, k_t, v_t, kk_t, a_t = inp
        sa = jnp.einsum('bhvk,bhk->bhv', S, kk_t)
        S = (S * w_t[:, :, None, :] - sa[..., None] * (kk_t * a_t)[:, :, None, :]
             + v_t[..., None] * k_t[:, :, None, :])
        return S, jnp.einsum('bhvk,bhk->bhv', S, r_t)

    tm = lambda t: jnp.moveaxis(t, 1, 0)
    S, o = lax.scan(step, S0, (tm(r), tm(decay), tm(k), tm(v), tm(kk), tm(a)))
    return S, jnp.moveaxis(o, 0, 1)

def _rwkv_group(p_rwkv, prev, S0, p):
    B, T, _ = p_rwkv.shape
    C = RWKV_WIDTH
    shifted = jnp.concatenate([prev[:, None].astype(p_rwkv.dtype), p_rwkv[:, :-1]], 1)
    z = (p_rwkv + p['mu'] * (shifted - p_rwkv)).astype(F32)
    r, k, v = z[..., :C], z[..., C:2 * C], z[..., 2 * C:3 * C]
    o0 = 3 * C
    wd = z[..., o0:o0 + DECAY_LORA]
    ad = z[..., o0 + DECAY_LORA:o0 + DECAY_LORA + AAA_LORA]
    gd = z[..., o0 + DECAY_LORA + AAA_LORA:]
    w_log = -jax.nn.softplus(-(p['w0'] + jnp.tanh(wd) @ p['w2'])) - 0.5
    decay = jnp.exp(-jnp.exp(w_log))
    a = jax.nn.sigmoid(p['a0'] + ad @ p['a2'])
    g = jax.nn.sigmoid(gd) @ p['g2']
    hs = lambda t: t.reshape(B, T, RWKV_HEADS, RWKV_HEAD)
    kk = hs(k * p['k_k'])
    kk = kk / jnp.maximum(jnp.sqrt(jnp.sum(kk * kk, -1, keepdims=True)), 1e-12)
    k = k * (1.0 + (a - 1.0) * p['k_a'])
    r, k, v, a, decay = hs(r), hs(k), hs(v), hs(a), hs(decay)
    S, o = _wkv_scan(S0.astype(F32), r, decay, k, v, kk, a)
    mu = jnp.mean(o, -1, keepdims=True)
    var = jnp.mean(jnp.square(o - mu), -1, keepdims=True)
    o = ((o - mu) * lax.rsqrt(var + GN_EPS)).reshape(B, T, C) * p['lnx_g'] + p['lnx_b']
    o = o + (jnp.sum(r * k * p['r_k'], -1, keepdims=True) * v).reshape(B, T, C)
    return o * g, S, p_rwkv[:, -1]

def _mla_project(p_mla, pos, p):
    B, T, _ = p_mla.shape
    cq = p_mla[..., :Q_RANK]
    ckv = p_mla[..., Q_RANK:Q_RANK + KV_RANK]
    kr = p_mla[..., Q_RANK + KV_RANK:]
    q = (_rmsnorm(cq, p['q_norm']) @ p['w_q_up']).reshape(B, T, MLA_HEADS, MLA_NOPE + MLA_ROPE)
    q_rope = _rope(q[..., MLA_NOPE:], pos)
    q_lat = jnp.einsum('bthn,rhn->bthr', q[..., :MLA_NOPE], p['w_uk'])
    lat = _rmsnorm(ckv, p['kv_norm'])
    return q_lat, q_rope, lat, _rope(kr, pos)

def _layer(x, c, pos, S0, prev, attend, p):
    mod = jax.nn.silu(c) @ p['w_ada'] + p['b_ada']
    sh1, sc1, g1, sh2, sc2, g2 = jnp.split(mod[:, None, :], 6, axis=-1)
    h = x * (1.0 + sc1) + sh1
    proj = h @ p['w_in']
    o_r, S, last = _rwkv_group(proj[..., :N_SHIFT], prev, S0, p)
    q_lat, q_rope, lat, kr = _mla_project(proj[..., N_SHIFT:], pos, p)
    ctx = attend(q_lat, q_rope, lat, kr)
    o_m = jnp.einsum('bthr,rhv->bthv', ctx, p['w_uv']).reshape(x.shape[0], x.shape[1], MLA_WIDTH)
    o_m = _rmsnorm(o_m, p['out_norm'])
    mixed = jnp.concatenate([o_r.astype(x.dtype), o_m.astype(x.dtype)], -1) @ p['w_out']
    x = _layernorm(DEEPNORM_ALPHA * x + g1 * mixed, p['ln1_g'], p['ln1_b'])
    h2 = x * (1.0 + sc2) + sh2
    f = jnp.square(jax.nn.relu(h2 @ p['w_up'])) @ p['w_down']
    x = _layernorm(DEEPNORM_ALPHA * x + g2 * f, p['ln2_g'], p['ln2_b'])
    return x, lat, kr, S, last

def setup_inputs(seed: int = 0) -> dict:
    key = jax.random.key(seed)
    ks = iter(jax.random.split(key, 48))
    nrm = lambda shape, s=1.0: s * jax.random.normal(next(ks), shape, F32)
    one = lambda shape: 1.0 + nrm(shape, 0.05)
    L = DEPTH
    n_pages = PAST_LEN // PAGE_SIZE
    n_pool = (DEC_BATCH * n_pages * 5) // 4
    page_table = jax.random.permutation(next(ks), n_pool)[:DEC_BATCH * n_pages]
    page_table = page_table.reshape(DEC_BATCH, n_pages).astype(jnp.int32)
    inp = {}
    inp['x_prompt'] = nrm((BATCH, SEQ, D_MODEL))
    inp['x_sample'] = nrm((DEC_BATCH, DEC_SEQ, D_MODEL))
    inp['c_prompt'] = nrm((BATCH, D_MODEL))
    inp['c_sample'] = nrm((DEC_BATCH, D_MODEL))
    inp['cache_latent'] = nrm((L, n_pool, PAGE_SIZE, KV_RANK))
    inp['cache_krope'] = nrm((L, n_pool, PAGE_SIZE, MLA_ROPE))
    inp['state_wkv'] = nrm((L, DEC_BATCH, RWKV_HEADS, RWKV_HEAD, RWKV_HEAD), 0.3)
    inp['state_shift'] = nrm((L, DEC_BATCH, N_SHIFT))
    inp['page_table'] = page_table
    inp['w_ada'] = nrm((L, D_MODEL, 6 * D_MODEL), D_MODEL ** -0.5)
    inp['b_ada'] = nrm((L, 6 * D_MODEL), 0.02)
    inp['w_in'] = nrm((L, D_MODEL, N_IN), D_MODEL ** -0.5)
    inp['rwkv_mu'] = jax.random.uniform(next(ks), (L, N_SHIFT), F32)
    inp['rwkv_w0'] = jax.random.uniform(next(ks), (L, RWKV_WIDTH), F32, -4.0, 1.0)
    inp['rwkv_w2'] = nrm((L, DECAY_LORA, RWKV_WIDTH), DECAY_LORA ** -0.5)
    inp['rwkv_a0'] = nrm((L, RWKV_WIDTH), 0.1)
    inp['rwkv_a2'] = nrm((L, AAA_LORA, RWKV_WIDTH), AAA_LORA ** -0.5)
    inp['rwkv_g2'] = nrm((L, GATE_LORA, RWKV_WIDTH), GATE_LORA ** -0.5)
    inp['rwkv_k_k'] = 0.85 + nrm((L, RWKV_WIDTH), 0.05)
    inp['rwkv_k_a'] = one((L, RWKV_WIDTH))
    inp['rwkv_r_k'] = nrm((L, RWKV_HEADS, RWKV_HEAD), 0.1)
    inp['rwkv_lnx_g'] = one((L, RWKV_WIDTH))
    inp['rwkv_lnx_b'] = nrm((L, RWKV_WIDTH), 0.02)
    inp['mla_q_norm'] = one((L, Q_RANK))
    inp['mla_w_q_up'] = nrm((L, Q_RANK, MLA_HEADS * (MLA_NOPE + MLA_ROPE)), Q_RANK ** -0.5)
    inp['mla_kv_norm'] = one((L, KV_RANK))
    inp['mla_w_uk'] = nrm((L, KV_RANK, MLA_HEADS, MLA_NOPE), KV_RANK ** -0.5)
    inp['mla_w_uv'] = nrm((L, KV_RANK, MLA_HEADS, MLA_V), KV_RANK ** -0.5)
    inp['mla_out_norm'] = one((L, MLA_WIDTH))
    inp['w_out'] = nrm((L, D_MODEL, D_MODEL), DEEPNORM_BETA * D_MODEL ** -0.5)
    inp['ln1_g'] = one((L, D_MODEL))
    inp['ln1_b'] = nrm((L, D_MODEL), 0.02)
    inp['w_up'] = nrm((L, D_MODEL, D_FF), D_MODEL ** -0.5)
    inp['w_down'] = nrm((L, D_FF, D_MODEL), DEEPNORM_BETA * D_FF ** -0.5)
    inp['ln2_g'] = one((L, D_MODEL))
    inp['ln2_b'] = nrm((L, D_MODEL), 0.02)
    return inp

def reference(x_prompt, x_sample, c_prompt, c_sample, cache_latent, cache_krope, state_wkv,
              state_shift, page_table, w_ada, b_ada, w_in, rwkv_mu, rwkv_w0, rwkv_w2, rwkv_a0,
              rwkv_a2, rwkv_g2, rwkv_k_k, rwkv_k_a, rwkv_r_k, rwkv_lnx_g, rwkv_lnx_b, mla_q_norm,
              mla_w_q_up, mla_kv_norm, mla_w_uk, mla_w_uv, mla_out_norm, w_out, ln1_g, ln1_b,
              w_up, w_down, ln2_g, ln2_b):
    B, T = x_prompt.shape[:2]
    Td = x_sample.shape[1]
    past = page_table.shape[1] * cache_latent.shape[2]
    pos_p = jnp.arange(T)
    pos_s = past + jnp.arange(Td)
    yp, ys = x_prompt, x_sample
    lat_p, kr_p, wkv_p, sh_p = [], [], [], []
    lat_s, kr_s, wkv_s, sh_s = [], [], [], []
    for l in range(DEPTH):
        p = dict(w_ada=w_ada[l], b_ada=b_ada[l], w_in=w_in[l], mu=rwkv_mu[l], w0=rwkv_w0[l],
                 w2=rwkv_w2[l], a0=rwkv_a0[l], a2=rwkv_a2[l], g2=rwkv_g2[l], k_k=rwkv_k_k[l],
                 k_a=rwkv_k_a[l], r_k=rwkv_r_k[l], lnx_g=rwkv_lnx_g[l], lnx_b=rwkv_lnx_b[l],
                 q_norm=mla_q_norm[l], w_q_up=mla_w_q_up[l], kv_norm=mla_kv_norm[l],
                 w_uk=mla_w_uk[l], w_uv=mla_w_uv[l], out_norm=mla_out_norm[l], w_out=w_out[l],
                 ln1_g=ln1_g[l], ln1_b=ln1_b[l], w_up=w_up[l], w_down=w_down[l],
                 ln2_g=ln2_g[l], ln2_b=ln2_b[l])
        S0 = jnp.zeros((B, RWKV_HEADS, RWKV_HEAD, RWKV_HEAD), F32)
        prev0 = jnp.zeros((B, N_SHIFT), x_prompt.dtype)
        yp, lp, kp, Sp, hp = _layer(yp, c_prompt, pos_p, S0, prev0, _prompt_attention, p)
        att_s = lambda ql, qr, ln, kn, cl=cache_latent[l], ck=cache_krope[l]: _sample_attention(
            ql, qr, ln, kn, cl, ck, page_table)
        ys, ls, kss, Ss, hs_ = _layer(ys, c_sample, pos_s, state_wkv[l], state_shift[l], att_s, p)
        lat_p.append(lp); kr_p.append(kp); wkv_p.append(Sp.astype(x_prompt.dtype)); sh_p.append(hp)
        lat_s.append(ls); kr_s.append(kss); wkv_s.append(Ss.astype(state_wkv.dtype)); sh_s.append(hs_)
    return (yp, ys, jnp.stack(lat_p), jnp.stack(kr_p), jnp.stack(wkv_p), jnp.stack(sh_p),
            jnp.stack(lat_s), jnp.stack(kr_s), jnp.stack(wkv_s), jnp.stack(sh_s))


_drawn_inputs = setup_inputs


def setup_inputs(seed=0):
    import zlib

    import numpy as np

    out = dict(_drawn_inputs(seed))
    spreads = {}
    factors = {'rwkv_lnx_g': 8.0,
     'rwkv_lnx_b': 41.26,
     'mla_q_norm': 5.461,
     'mla_out_norm': 5.234,
     'ln1_b': 2.86,
     'ln2_b': 2.906}
    for name, (base, spread) in spreads.items():
        noise = np.random.default_rng([zlib.crc32(name.encode()), seed]).standard_normal(out[name].shape)
        drawn = base * np.exp(spread * noise) if base else spread * noise
        out[name] = __import__('jax').numpy.asarray(drawn.astype(out[name].dtype))
    for name, factor in factors.items():
        out[name] = (out[name] * factor).astype(out[name].dtype)
    return out
```

```python
from contextlib import ExitStack

import concourse.bass as bass
import numpy as np
from concourse import mybir
from concourse.alu_op_type import AluOpType as ALU

ACT = mybir.ActivationFunctionType
AX = mybir.AxisListType
F32 = mybir.dt.float32
I32 = mybir.dt.int32
F22 = mybir.dt.float32r

P = 128
D = 2048
KT = D // P
NP_TOK, NS, TS = 256, 8, 4
NTOK = NP_TOK + NS * TS
RW = 1024
RT = RW // P
HD = 64
LORA, GLORA = 96, 256
N_SHIFT = 3 * RW + 2 * LORA + GLORA
MH, NOPE, ROPE, QR, KVR = 8, 128, 64, 512, 256
QH = NOPE + ROPE
N_IN = N_SHIFT + QR + KVR + ROPE
FF = 8192
PAGE, NPAGES = 128, 16
CH, NCH = 64, NP_TOK // 64
ALPHA = 2.0 ** 0.25
DECAY_C = float(np.exp(-0.5))
SM_SCALE = float(QH) ** -0.5
LN_EPS, RMS_EPS, GN_EPS = 1e-5, 1e-6, 64e-5
SLAB_COLS = 256
RING = 4
NEG = -1e30

C_ID, C_ONE, C_BLK = 0, 128, 256
C_M2, C_M2T, C_LVL = 384, 512, 640
C_AR = C_LVL + 5 * 128
C_SCAN = C_AR + 128
C_COS, C_SIN = C_SCAN + NTOK, C_SCAN + 2 * NTOK
C_ROT = C_SCAN + 3 * NTOK
C_CAUS = C_ROT + 64
C_NEW = C_CAUS + 128
C_SEL = C_NEW + 64
C_SEQ = C_SEL + 9
C_ARS = C_SEQ + 8
C_END = C_ARS + 64


def shape_constants():
    t = np.zeros((P, C_END), np.float32)
    i = np.arange(P)
    t[:, C_ID:C_ID + P] = np.eye(P)
    t[:, C_ONE:C_ONE + P] = 1.0
    t[:, C_BLK:C_BLK + P] = i[:, None] // HD == i[None] // HD
    r, c = i[:, None], i[None]
    strict2 = (r // 2 == c // 2) & (c < r)
    t[:, C_M2:C_M2 + P] = strict2
    t[:, C_M2T:C_M2T + P] = strict2.T
    for n, b in enumerate((2, 4, 8, 16, 32)):
        t[:, C_LVL + n * P:C_LVL + (n + 1) * P] = (
            (r // (2 * b) == c // (2 * b)) & (r // b % 2 == 0) & (c // b % 2 == 1))
    s64, t64 = i[:, None] % 64, np.arange(64)[None]
    t[:, C_AR:C_AR + 64] = s64 < t64
    t[:, C_AR + 64:C_AR + 128] = s64 <= t64
    scan = np.ones(NTOK)
    scan[0:NP_TOK:CH] = 0
    scan[NP_TOK::TS] = 0
    t[:, C_SCAN:C_SCAN + NTOK] = scan
    pos = np.concatenate([np.arange(NP_TOK), np.tile(PAGE * NPAGES + np.arange(TS), NS)]).astype(np.float32)
    inv = (10000.0 ** (-np.arange(32) / 32)).astype(np.float32)
    ang = (pos[None] * inv[:, None]).astype(np.float32)
    for q in range(2):
        t[32 * q:32 * q + 32, C_COS:C_COS + NTOK] = np.cos(ang)
        t[32 * q:32 * q + 32, C_SIN:C_SIN + NTOK] = np.sin(ang)
    for m in range(32):
        t[m + 32, C_ROT + m] = -1.0
        t[m, C_ROT + 32 + m] = 1.0
    t[:, C_CAUS:C_CAUS + P] = np.where(c <= r, 0.0, NEG)
    for g in range(2):
        col = np.arange(32)[None]
        ok = (col // TS == 4 * g + r // 32) & (col % TS <= r % TS)
        t[:, C_NEW + 32 * g:C_NEW + 32 * g + 32] = np.where(ok, 0.0, NEG)
    t[:, C_SEL:C_SEL + 9] = i[:, None] % 32 == np.arange(9)[None]
    t[:, C_SEQ:C_SEQ + 8] = i[:, None] % 32 // TS == np.arange(8)[None]
    s32, t32 = i[:, None] % 32, np.arange(32)[None]
    same = s32 // TS == t32 // TS
    t[:, C_ARS:C_ARS + 32] = same & (s32 < t32)
    t[:, C_ARS + 32:C_ARS + 64] = same & (s32 <= t32)
    return t


EW_MARKS, TILE_MARKS = 2, 16
(PE_A4, PE_BK, PE_RV, PE_SMP, PE_AR, PE_S0, PE_BON, PE_YS, PE_DS, PE_TS, PE_XS, PE_US, PE_OS, PE_SN, PE_O, PE_SNT, PE_STT) = range(1, 18)
PE_N = 17
(ACT_A4, ACT_BK, ACT_SMP, ACT_S0, ACT_YS, ACT_US, ACT_O, ACT_SNT, ACT_STT) = range(1, 10)
ACT_N = 9
(DVE_RV, DVE_NTS, DVE_AR, DVE_BON, DVE_DS, DVE_TS, DVE_XS, DVE_OS, DVE_SN) = range(1, 10)
DVE_N = 9

ADA0, N_ADA = 0, 16
N_LATE = 32
WIN0 = N_ADA
N_RKV = 12
LOR = WIN0 + 18
QUP = LOR + 1
WUK = QUP + 2
CACHE0 = WUK + 1
OUT0, N_OUT = CACHE0 + NS, 8
UP0, N_UP = OUT0 + N_OUT, 32
DN0, N_DN = UP0 + N_UP, 32
SLAB_DMAS = {LOR: 3, QUP: 1 + N_LATE // 2, QUP + 1: 1 + N_LATE // 2,
             **{CACHE0 + s: NPAGES for s in range(NS)}}


def slab_ready(n):
    return 16 * sum(SLAB_DMAS.get(m, 1) for m in range(n % RING, n + 1, RING))


class Chain:

    def __init__(self, eng, sem):
        self.eng, self.sem, self.base, self.k, self.it = eng, sem, 0, 0, None

    def value(self):
        return self.k + self.base if self.it is None else self.it * self.per + (self.base + self.k)

    def mark(self, ins):
        ins.then_inc(self.sem, 1)
        self.k += 1

    def wait(self):
        self.eng.wait_ge(self.sem, self.value())

    def link(self, ins):
        self.mark(ins)
        self.wait()

    def enter(self, it, per):
        self.base, self.k, self.it, self.per = self.base + self.k, 0, it, per

    def leave(self, times):
        assert self.k == self.per, (self.k, self.per)
        self.base, self.k, self.it = self.base + times * self.per, 0, None


ARENA = 23616
LATE = 22112


def build(nc, a, dbg=None):
    ctx = ExitStack()
    with ctx:
        def sb(name, cols, dtype=F32, scope=ctx):
            return scope.enter_context(nc.sbuf_tensor(name, [P, cols], dtype))

        def sem(name):
            return ctx.enter_context(nc.semaphore(name))

        const = sb("const", C_END)
        par = sb("par", 272)
        eps = sb("eps", 3)
        xT = sb("xT", KT * NTOK)[:, :].rearrange("p (k n) -> p k n", k=KT)
        mod = sb("mod", 96 * 9)[:, :].rearrange("p (k n) -> p k n", k=96)
        page_ids = ctx.enter_context(nc.sbuf_tensor("page_ids", [1, NS * NPAGES], I32))
        bank = [ctx.enter_context(nc.psum_tensor(f"bank{i}", [P, 512], F32)) for i in range(8)]
        with ExitStack() as whole:
            ring = [sb(f"slab{i}", KT * SLAB_COLS, scope=whole) for i in range(RING)]
            hT_m = sb("hT", KT * NTOK, scope=whole)
            arena = sb("arena", ARENA, scope=whole)
        with ExitStack() as parts:
            ring_lo = [sb(f"slab_lo{i}", KT * SLAB_COLS, F22, parts) for i in range(RING)]
            hT_lo_m = sb("hT_lo", KT * NTOK, F22, parts)
            arena_hi = sb("arena_hi", ARENA, F22, parts)
        slab = [r[:, :].rearrange("p (k c) -> p k c", k=KT) for r in ring]
        slab_lo = [r[:, :].rearrange("p (k c) -> p k c", k=KT) for r in ring_lo]
        hT, hT_lo = (v[:, :].rearrange("p (k n) -> p k n", k=KT) for v in (hT_m, hT_lo_m))

        def carve(start, *dims, of=arena):
            n = int(np.prod(dims))
            v = of[:, start:start + n]
            if len(dims) == 2:
                v = v.rearrange("p (a b) -> p a b", a=dims[0])
            if len(dims) == 3:
                v = v.rearrange("p (a b c) -> p a b c", a=dims[0], b=dims[1])
            assert start + n <= ARENA, (start + n, ARENA)
            return v, start + n

        z, o = carve(0, 24, NTOK)
        mla, MLA_END = carve(o, 7, NTOK)
        sigw, o = carve(MLA_END, RT, NTOK)
        ag, SIG_END = carve(o, RT, NTOK)
        zl, o = carve(SIG_END, 4, NTOK)
        pad, o = carve(o, 2, 1 + NP_TOK + NS * 5)
        dif, o = carve(o, 2, 296)
        last, o = carve(o, 28, 9)
        shT, o = carve(o, 28, NS)
        LAST_ROWS = o
        last_rows, LAST_END = carve(o, 1, 28 * P)
        sq, o = carve(SIG_END + 4 * NTOK, 2, NTOK)
        nrm, o = carve(o, 2, NTOK)
        lora = ring[LOR % RING]
        w2_v, a2_v = lora[0:LORA, 0:RW], lora[0:LORA, RW:2 * RW]
        g2_v = lora[:, 2 * RW:4 * RW].rearrange("p (k c) -> p k c", k=2)
        gnv, o = carve(o, 2, NTOK)
        dif288, o = carve(o, NTOK)
        assert o <= ARENA
        xrow, o = carve(0, 3, D)
        crow, o = carve(o, 3, D)
        shrow, _ = carve(LAST_ROWS, N_SHIFT)
        prow, o = carve(LAST_END, 3, P)
        cT, o = carve(LATE, KT * 9 + 32)
        part, o = carve(o, 4, SLAB_COLS)

        lam, o = carve(SIG_END, NTOK)
        dec, o = carve(o, 3, NTOK)
        kka, o = carve(o, NTOK)
        kmul, o = carve(o, NTOK)
        rkk, o = carve(o, NTOK)
        ew_buf = []
        for u in range(2):
            abr, o = carve(o, 3, NTOK)
            bk, o = carve(o, NCH * P + 64)
            rv, o = carve(o, NCH * P + 64)
            pend, o = carve(o, NCH + NS)
            ew_buf.append((abr, bk, rv, pend))
        bkT, o = carve(o, NCH, P)
        uv, o = carve(o, NCH, P)
        st, o = carve(o, 2, HD)
        st_dec, o = carve(o, HD)
        d_sb, o = carve(o, P)
        omka, o = carve(o, RT)
        a4, o = carve(o, 8, P)
        arS = []
        for u in range(2):
            v, o = carve(o, 64)
            arS.append(v)
        assert o <= LATE

        def carve_slot(s, start, *dims):
            n = int(np.prod(dims))
            v = ring[s][:, start:start + n]
            if len(dims) == 2:
                v = v.rearrange("p (a b) -> p a b", a=dims[0])
            if len(dims) == 3:
                v = v.rearrange("p (a b c) -> p a b c", a=dims[0], b=dims[1])
            assert start + n <= KT * SLAB_COLS
            return v, start + n
        slot = (WIN0 + 17) % RING
        ar, o = carve_slot(slot, 0, 2 * NCH, P)
        nt, o = carve_slot(slot, o, 8, P)
        nt_v = [nt[:, 0:4, :], nt[:, 4:8, :]]
        tm, o = carve_slot(slot, o, 4, P)
        tt, o = carve_slot(slot, o, 4, P)
        y_sb, o = carve_slot(slot, o, 4, P)
        slot = LOR % RING
        s0n, o = carve_slot(slot, 0, 4, P)
        s1n, o = carve_slot(slot, o, 4, P)
        s0t, o = carve_slot(slot, o, 4, P)
        uve, o = carve_slot(slot, o, 2, 512)
        bks, o = carve_slot(slot, o, P)
        uvs, o = carve_slot(slot, o, P)
        ars, o = carve_slot(slot, o, 2, 64)
        ts_m, o = carve_slot(slot, o, 2, 32)
        ts_t, o = carve_slot(slot, o, 2, 32)
        ts_n, o = carve_slot(slot, o, 2, 32)
        ts_y, o = carve_slot(slot, o, 2, 32)
        ds, o = carve_slot(slot, o, 2, 64)
        d_smp, o = carve_slot(slot, o, P)
        o_smp, o = carve_slot(slot, o, P)
        sto, o = carve_slot(slot, o, P)

        qlT, o = carve(MLA_END, 2 * MH, NTOK)
        qlT = qlT.rearrange("p (r h) n -> p r h n", r=2)
        qrT, o = carve(o, MH, NTOK)
        latT, o = carve(o, 2, NTOK)
        krT, o = carve(o, NTOK)
        latN, o = carve(o, 3, KVR)
        w_uv, KR_PAGES = carve(o, 2, MH * P)
        ukT, o = carve(KR_PAGES, MH, KVR)
        cqn, o = carve(o, 4, NTOK)
        rin, o = carve(o, 2, NTOK)
        krN = hT[:, KT - 1, :]
        sqm, o = carve(0, 6, NTOK)
        qn, o = carve(o, 2, NTOK)
        qraw, o = carve(o, 2, NTOK)
        rot_a, o = carve(o, NTOK)
        rot_b, o = carve(o, NTOK)
        S, o = carve(0, 2080)
        latS, o = carve(o, 4, 2 * 256)
        krS, o = carve(o, 2, 512)
        pT, o = carve(o, 17, P)
        S2, o = carve(o, 2, 256)
        pT2, o = carve(o, 2, 256)
        sm, o = carve(o, 16)
        MISC = o
        qs, o = carve(o, 2, NS * 32)
        qrs = S2.rearrange("p a b -> p (a b)")[:, 0:NS * 32]
        ctxs = pT2[:, 0, :]
        assert o <= MLA_END
        kr_pages, _ = carve(KR_PAGES, 4, NPAGES * ROPE)
        osq, _ = carve(15840, 2, NTOK)
        w_hi, o = carve(0, 2, KT, P, of=arena_hi)
        o_hi, _ = carve(4320, KT, NTOK, of=arena_hi)
        f_hi, o = carve(o, KT, NTOK, of=arena_hi)
        f_lo, o = carve(o, KT, NTOK, of=arena_hi)
        lnb, o = carve(o, 8, NTOK)
        relu, o = carve(o, 2, NTOK)
        relu_sq, o = carve(o, 2, NTOK)
        x_hi, o = carve(o, KT, NTOK, of=arena_hi)
        y_rows, _ = carve(0, 3, D)

        ident = const[:, C_ID:C_ID + P]
        ones = const[:, C_ONE:C_ONE + P]
        blk = const[:, C_BLK:C_BLK + P]

        slab_in = [sem(f"slab_in{i}") for i in range(RING)]
        const_in, par_in, c_in, x_in, shift_in = (sem(s) for s in ("const_in", "par_in", "c_in", "x_in", "shift_in"))
        padded = sem("padded")
        c_sig, c_silu, c_turned, c_ready = (sem(s) for s in ("c_sig", "c_silu", "c_turned", "c_ready"))
        par_turned, par_ready = sem("par_turned"), sem("par_ready")
        sh_turned, sh_ready = sem("sh_turned"), sem("sh_ready")
        x_turned, x_ready = sem("x_turned"), sem("x_ready")
        ada_mm, ada_part, ada_sum, mod_ready = (sem(s) for s in ("ada_mm", "ada_part", "ada_sum", "mod_ready"))
        h_ready = sem("h_ready")
        win_mm, win_copied, z_ready, last_ready = (sem(s) for s in ("win_mm", "win_copied", "z_ready", "last_ready"))
        last_turned, last_out, stored = sem("last_turned"), sem("last_out"), sem("stored")
        act_step, dve_step, pool_step = sem("act_step"), sem("dve_step"), sem("pool_step")

        lora_turned = sem("lora_turned")
        lora_mm, lora_sig, g_ready = sem("lora_mm"), sem("lora_sig"), sem("g_ready")
        kk_raw, kk_sq, kk_mm, kk_nrm, kk_ready = (sem(s) for s in ("kk_raw", "kk_sq", "kk_mm", "kk_nrm", "kk_ready"))
        (ew_scan, ew_lp, ew_exp, ew_pool, ew_v, ew_a, ew_kv, ew_rk) = (
            sem("ew_" + s) for s in ("scan", "lp", "exp", "pool", "v", "a", "kv", "rk"))
        pe_tile, act_tile, dve_tile = sem("pe_tile"), sem("act_tile"), sem("dve_tile")
        p_y, p_inc, p_d, p_x, p_u, p_s = (sem("pe_" + s) for s in ("y", "inc", "d", "x", "u", "s"))
        e_t, e_nt, e_y, e_uve, e_d, e_u, e_st = (sem("got_" + s) for s in ("t", "nt", "y", "uve", "d", "u", "st"))
        s0_in, state_out = sem("s0_in"), sem("state_out")

        gn_sq, gn_mm, gn_var, gn_std, gn_cen, gn_nrm, gn_ready = (sem("gn_" + s) for s in (
            "sq", "mm", "var", "std", "cen", "nrm", "ready"))
        uv_in = sem("uv_in")
        m_sq, m_mm, m_std, m_ready, kr_ready = (sem("mla_" + s) for s in ("sq", "mm", "std", "ready", "kr"))
        uk_turned, uk_ready = sem("uk_turned"), sem("uk_ready")
        q_mm, q_copied, q_rot, qr_ready, ql_mm, ql_ready = (sem("q_" + s) for s in ("mm", "copied", "rot", "rope", "lat_mm", "lat"))
        lat_turned, lat_rows = sem("lat_turned"), sem("lat_rows")
        pa_s, pa_max, pa_exp, pa_p, pa_T, pa_pT, pa_ctx, pa_ready = (sem("pa_" + s) for s in (
            "s", "max", "exp", "p", "T", "pT", "ctx", "ready"))
        qs_ready = sem("qs_ready")
        kr_in = [sem(f"kr_in{i}") for i in range(4)]
        ids_in = sem("ids_in")
        (sa_tr, sa_lat, sa_kr, sa_s, sa_copied, sa_max, sa_exp, sa_T, sa_pT, sa_ctx, sa_ctx_n, sa_ctxT, sa_ready, sa_rinv) = (
            sem("sa_" + s) for s in ("tr", "lat", "kr", "s", "copied", "max", "exp", "T", "pT", "ctx", "ctx_n", "ctxT", "ready", "rinv"))
        om_mm, om_sq, om_sum, om_std, om_ready = (sem("om_" + s) for s in ("mm", "sq", "sum", "std", "ready"))
        xa_ready = sem("xa_ready")
        w_split, h_split, f_split, tile_mm, x_added = (sem(s) for s in ("w_split", "h_split", "f_split", "tile_mm", "x_added"))
        x_sq, x_acc1, x_acc2 = sem("x_sq"), sem("x_acc1"), sem("x_acc2")
        ln_mm, ln_var, ln_std, ln_rstd, ln_cen, ln_nrm, ln_x = (sem("ln_" + s) for s in ("mm", "var", "std", "rstd", "cen", "nrm", "x"))
        h2_ready, xa2_ready = sem("h2_ready"), sem("xa2_ready")
        up_relu, up_f = sem("up_relu"), sem("up_f")
        y_T, y_rows_a, y_rows_d = sem("y_T"), sem("y_rows_a"), sem("y_rows_d")

        passed = {mybir.EngineType.PE: sem("pe_passed"), mybir.EngineType.Pool: sem("pool_passed")}

        NWIN = 35

        slab_free = {n: (ada_mm, n + 1) for n in range(N_ADA)}
        slab_free |= {WIN0 + n: (win_mm, min(2 * n + 2, NWIN)) for n in range(18)}

        slab_free[QUP], slab_free[QUP + 1] = (q_mm, 5), (q_mm, MH)
        slab_free[WUK] = (uk_turned, 4)
        slab_free |= {CACHE0 + n: (sa_ctx, 1 + n // 4) for n in range(NS)}
        LATE_SLOTS = [QUP % RING, (QUP + 1) % RING]
        slab_free[LOR] = (act_tile, (RT - 1) * ACT_N + ACT_O)
        slab_free[LOR - 1] = (act_tile, (RT - 1) * ACT_N + ACT_O)

        def pairs(eng, body, times=RT // 2):
            for u in range(2):
                body(u, u)
            with eng.Fori(1, times) as i:
                for u in range(2):
                    body(i * 2 + u, u)

        def first(j):
            return isinstance(j, int) and j == 0

        def wait(eng, sem_, value):
            eng.wait_ge(sem_, value)
            if not isinstance(value, int):
                eng.sem_inc(passed[eng.engine], 1)

        block = ctx.enter_context(nc.Block())

        @block.sync
        def _(sp):
            w_ada = a["w_ada"][0].rearrange("(k p) c -> p k c", p=P)
            for n in range(RING):
                sp.dma_start(slab[n], w_ada[:, :, n * SLAB_COLS:(n + 1) * SLAB_COLS]).then_inc(slab_in[n], 16)
            with sp.Fori(1, N_ADA // RING) as i:
                for u in range(RING):
                    sp.wait_ge(ada_mm, i * RING + (u + 1 - RING))
                    sp.dma_start(slab[u], w_ada[:, :, bass.ds(i * (RING * SLAB_COLS) + u * SLAB_COLS, SLAB_COLS)]
                                 ).then_inc(slab_in[u], 16)
            w_in = a["w_in"][0].rearrange("(k p) c -> p k c", p=P)

            def wait_free(n):
                used, value = slab_free[n - RING]
                sp.wait_ge(used, value)

            def load_win(n, c0, w):
                wait_free(n)
                sp.dma_start(slab[n % RING][:, :, 0:w], w_in[:, :, c0:c0 + w]).then_inc(slab_in[n % RING], 16)
            load_win(WIN0, 3 * RW, 2 * LORA)
            load_win(WIN0 + 1, 3 * RW + 2 * LORA, GLORA)

            def win_rkv(i, u):
                s = (WIN0 + 2 + u) % RING
                sp.dma_start(slab[s], w_in[:, :, bass.ds(i * (RING * SLAB_COLS) + u * SLAB_COLS, SLAB_COLS)]
                             ).then_inc(slab_in[s], 16)
            for u in range(RING):
                wait_free(WIN0 + 2 + u)
                win_rkv(0, u)
            with sp.Fori(1, N_RKV // RING) as i:
                for u in range(RING):
                    sp.wait_ge(win_mm, i * 2 * RING + (4 + 2 * (u + 1) - 2 * RING))
                    win_rkv(i, u)
            for m in range(3):
                load_win(WIN0 + 14 + m, N_SHIFT + SLAB_COLS * m, SLAB_COLS)
            load_win(WIN0 + 17, N_SHIFT + QR + KVR, ROPE)
            s = LOR % RING
            wait_free(LOR)
            sp.dma_start(w2_v, a["rwkv_w2"][0]).then_inc(slab_in[s], 16)
            sp.dma_start(a2_v, a["rwkv_a2"][0]).then_inc(slab_in[s], 16)
            sp.dma_start(g2_v, a["rwkv_g2"][0].rearrange("(k p) c -> p k c", p=P)).then_inc(slab_in[s], 16)
            def load_late(j, c, after):
                if after is not None:
                    sp.wait_ge(ada_mm, after)
                s = LATE_SLOTS[c % 2]
                sp.dma_start(slab[s], w_ada[:, :, bass.ds(j * (4 * SLAB_COLS) + (N_ADA + c) * SLAB_COLS, SLAB_COLS)]).then_inc(slab_in[s], 16)
            for c in range(2):
                wait_free(QUP + c)
                load_late(0, c, None)
            sp.wait_ge(last_out, 7)
            sp.dma_start(a["new_shift_prompt"], last_rows[0:1, 0, 0:N_SHIFT]).then_inc(stored, 16)
            sp.dma_start(a["new_shift_sample"][0], last_rows[1:9, 0, 0:N_SHIFT]).then_inc(stored, 16)
            s_in = a["state_wkv"][0].rearrange("(q e) h v k -> e v q h k", e=2)
            s_out = a["new_wkv_sample"][0].rearrange("(q e) h v k -> e v q h k", e=2)
            p_out = a["new_wkv_prompt"][0, 0].rearrange("h v k -> v h k")
            sp.wait_ge(lora_mm, 2 * RT)
            def state_in(j):
                for e in range(2):
                    for q in range(4):
                        sp.dma_start(s0n[64 * e:64 * e + 64, q, :].rearrange("p (h k) -> p h k", h=2),
                                     s_in[e, :, q, bass.ds(j * 2, 2), :]).then_inc(s0_in, 16)

            def out_states(j):
                sp.wait_ge(act_tile, j * ACT_N + ACT_SNT)
                for e in range(2):
                    for q in range(4):
                        sp.dma_start(s_out[e, :, q, bass.ds(j * 2, 2), :],
                                     s1n[64 * e:64 * e + 64, q, :].rearrange("p (h k) -> p h k", h=2)).then_inc(state_out, 16)
                sp.wait_ge(act_tile, j * ACT_N + ACT_STT)
                sp.dma_start(p_out[:, bass.ds(j * 2, 2), :], sto[0:64, :].rearrange("p (h k) -> p h k", h=2)
                             ).then_inc(state_out, 16)
            state_in(0)
            with sp.Fori(0, RT - 1) as j:
                sp.wait_ge(pe_tile, j * PE_N + PE_S0)
                state_in(j + 1)
                for c in range(4):
                    load_late(j, c + 2, j * 4 + (N_ADA + c + 1))
                out_states(j)
            for c in range(2):
                load_late(RT - 1, c + 2, (RT - 1) * 4 + N_ADA + c + 1)
            qup = a["mla_w_q_up"][0].rearrange("(k p) c -> p k c", p=P)
            quv = [slab[(QUP + n) % RING].rearrange("p k c -> p (k c)").rearrange("p (k c) -> p k c", k=4) for n in range(2)]
            for n, (h0, nh) in enumerate(((0, 5), (5, 3))):
                sp.wait_ge(ada_mm, N_ADA + N_LATE - 1 + n)
                sp.dma_start(quv[n][:, :, 0:nh * QH], qup[:, :, h0 * QH:(h0 + nh) * QH]).then_inc(slab_in[(QUP + n) % RING], 16)
            out_states(RT - 1)
            sp.wait_ge(state_out, 16 * 9 * RT)
            s = WUK % RING
            wait_free(WUK)
            sp.wait_ge(e_t, 6 * RT)
            sp.wait_ge(pe_tile, (RT - 1) * PE_N + PE_STT)
            sp.dma_start(ring[s][:, 0:2 * MH * NOPE].rearrange("p (k c) -> p k c", k=2),
                         a["mla_w_uk"][0].rearrange("(k p) h n -> p k (h n)", p=P)).then_inc(slab_in[s], 16)
            sp.dma_start(w_uv, a["mla_w_uv"][0].rearrange("(k p) h n -> p k (h n)", p=P)).then_inc(uv_in, 16)
            sp.wait_ge(ids_in, 16)
            for q in range(NS):
                n, s = CACHE0 + q, (CACHE0 + q) % RING
                wait_free(n)
                with sp.Fori(0, NPAGES // 4) as g:
                    _, pages = nc.values_load_multi_w_load_instructions(
                        page_ids[0:1, bass.ds(g * 4 + q * NPAGES, 4)], engines=[mybir.EngineType.SP], min_val=0, max_val=a["cache_latent"].shape[1] - 1)
                    for e, page in enumerate(pages):
                        sp.dma_start(slab[s][:, bass.ds(g * 4 + e, 1), :].rearrange("p o c -> p (o c)"),
                                     a["cache_latent"][0][bass.ds(page, 1), :, :].rearrange("o p c -> (o p) c")).then_inc(slab_in[s], 16)
                if q == 0:
                    sp.wait_ge(lat_rows, 4)
                    for t in range(2):
                        rows = slice(t * P, (t + 1) * P)
                        sp.dma_start(a["new_latent_prompt"][0, 0, rows, :], latN[:, t, :]).then_inc(stored, 16)
                        sp.dma_start(a["new_krope_prompt"][0, 0, rows, :], krN[:, 64 * t:64 * t + 64]).then_inc(stored, 16)
                    sp.dma_start(a["new_latent_sample"][0].rearrange("s t c -> (s t) c"), latN[0:32, 2, :]).then_inc(stored, 16)
                    sp.dma_start(a["new_krope_sample"][0].rearrange("s t c -> (s t) c"), krN[0:32, 128:192]).then_inc(stored, 16)
            w_out = a["w_out"][0].rearrange("(k p) c -> p k c", p=P)
            w_up = a["w_up"][0].rearrange("(k p) c -> p k c", p=P)
            w_dn = a["w_down"][0].rearrange("(q k p) c -> p q k c", p=P, k=KT)

            def load(i, u, src):
                s = (OUT0 + u) % RING
                sp.wait_ge(tile_mm, i * 2 * RING + (2 * (u + 1) - 2 * RING))
                sp.dma_start(slab[s], src).then_inc(slab_in[s], 16)
            for u in range(RING):
                wait_free(OUT0 + u)
                sp.dma_start(slab[(OUT0 + u) % RING], w_out[:, :, u * SLAB_COLS:(u + 1) * SLAB_COLS]).then_inc(slab_in[(OUT0 + u) % RING], 16)
            for u in range(RING):
                load(1, u, w_out[:, :, (RING + u) * SLAB_COLS:(RING + u + 1) * SLAB_COLS])
            with sp.Fori(0, 4) as q:
                for m in range(8):
                    load(q * 4 + (2 + m // RING), m % RING, w_up[:, :, bass.ds(q * D + m * SLAB_COLS, SLAB_COLS)])
                for m in range(8):
                    load(q * 4 + (4 + m // RING), m % RING,
                         w_dn[:, bass.ds(q, 1), :, m * SLAB_COLS:(m + 1) * SLAB_COLS].rearrange("p o k c -> p (o k) c"))
            for n in range(12):
                g, q = n // 3, n % 3
                rows, cols = (P, slice(g * 512, (g + 1) * 512)) if q < 2 else (32, slice(g * 512, (g + 1) * 512))
                sp.wait_ge(y_rows_a if n % 2 else y_rows_d, n // 2 + 1)
                dst = a["y_prompt"][0, q * P:(q + 1) * P, cols] if q < 2 else a["y_sample"].rearrange("b t d -> (b t) d")[:, cols]
                sp.dma_start(dst, y_rows[0:rows, q, cols]).then_inc(stored, 16)
            sp.wait_ge(stored, 16 * (2 + 6 + 12))
        @block.gpsimd
        def _(pool):
            ch = Chain(pool, pool_step)
            for n, e in enumerate((GN_EPS, RMS_EPS, LN_EPS)):
                pool.memset(eps[:, n:n + 1], e)
            pool.memset(prow[:, :, :], 0.0).then_inc(padded, 1)
            pool.memset(cT, 0.0).then_inc(padded, 1)
            pool.memset(pad[:, :, 0:1], 0.0).then_inc(padded, 1)

            def keep_last(mt, par_, col, w):
                wait(pool, win_copied, mt + 1)
                pool.tensor_copy(last[0:w, bass.ds(col, 1), 0:1], pad[0:w, par_:par_ + 1, NP_TOK:NP_TOK + 1])
                pool.tensor_copy(last[0:w, bass.ds(col, 1), 1:9],
                                 pad[0:w, par_:par_ + 1, NP_TOK + 1 + 4:NP_TOK + 1 + 40:5]).then_inc(last_ready, 1)
            pool.wait_ge(padded, 3)
            for mt, (col, w) in enumerate([(24, LORA), (25, LORA), (26, P), (27, P)]):
                keep_last(mt, mt % 2, col, w)
            with pool.Fori(0, 3) as i:
                for m in range(8):
                    keep_last(i * 8 + (4 + m), m % 2, i * 8 + m, P)
            wait(pool, z_ready, 28)
            for j in range(RT):
                wait(pool, win_mm, NWIN)
                pool.tensor_scalar(hT[:, j, :], z[:, 8 + j, :], par[:, 128 + 16 + j:128 + 17 + j], None, ALU.mult).then_inc(kk_raw, 1)

            def tile_of(v, j):
                return v[:, bass.ds(j, 1), :].rearrange("p o n -> p (o n)")

            def chunks(v):
                return v.rearrange("p (c t) -> p c t", c=NCH)

            def elementwise(j, u):
                abr, bk, rv, pend = ew_buf[u]
                bk_p = bk[:, 0:NCH * P].rearrange("p (c n) -> p c n", c=NCH)
                wait(pool, ew_scan, j + 1)
                pool.tensor_tensor(tile_of(sigw, j), lam, tile_of(sigw, j), ALU.subtract).then_inc(ew_lp, 1)
                wait(pool, lora_sig, 2 * RT)
                wait(pool, kk_ready, RT)
                if not (isinstance(j, int) and j < 2):
                    wait(pool, pe_tile, j * PE_N + (PE_O - 2 * PE_N))
                ch.link(pool.tensor_tensor(kka, tile_of(hT, j), tile_of(ag, j), ALU.mult))
                wait(pool, ew_exp, j + 1)
                ch.mark(pool.tensor_tensor(abr[:, 1, :], kka, dec[:, 1, :], ALU.mult))
                wait(pool, ch.sem, ch.value())
                pool.tensor_copy(bk_p[:, :, 0:CH], chunks(abr[:, 1, 0:NP_TOK]))
                pool.tensor_copy(bk[:, NCH * P:NCH * P + 32], abr[:, 1, NP_TOK:NTOK])
                pool.tensor_tensor(tile_of(z, j + 8), tile_of(z, j + 8), kmul, ALU.mult).then_inc(ew_kv, 1)
                wait(pool, ew_kv, j + 1)
                kv = tile_of(z, j + 8)
                pool.tensor_tensor(bk_p[:, :, CH:P], chunks(kv[:, 0:NP_TOK]), chunks(dec[:, 1, 0:NP_TOK]), ALU.mult)
                pool.tensor_tensor(bk[:, NCH * P + 32:NCH * P + 64], kv[:, NP_TOK:NTOK], dec[:, 1, NP_TOK:NTOK], ALU.mult)
                pool.tensor_copy(pend[:, 0:NCH], dec[:, 0, CH - 1:NP_TOK:CH])
                pool.tensor_copy(pend[:, NCH:NCH + NS], dec[:, 0, NP_TOK + TS - 1:NTOK:TS])
                pool.tensor_tensor(abr[:, 2, :], tile_of(z, j), dec[:, 0, :], ALU.mult).then_inc(ew_pool, 1)

            def joins(j, n):
                if n == 0:
                    wait(pool, act_tile, j * ACT_N + ACT_A4)
                if n >= 2:
                    wait(pool, p_y, j * 5 + (n - 1))
                elif not first(j):
                    wait(pool, p_y, j * 5)
                pool.tensor_tensor(nt_v[n % 2].rearrange("p (h q) t -> p h q t", h=2), a4.rearrange("p (h w q) t -> p h w q t", h=2, w=2)[:, :, 1],
                                   const[:, C_LVL + n * P:C_LVL + (n + 1) * P].rearrange("p (a b t) -> p a b t", a=1, b=1).to_broadcast([P, 2, 2, P]),
                                   ALU.mult).then_inc(e_nt, 1)

            def tile(j, u, ahead=True):
                for n in range(5):
                    joins(j, n)
                if ahead:
                    elementwise(j + 1, 1 - u)
                wait(pool, act_tile, j * ACT_N + ACT_US)
                wait(pool, dve_tile, j * DVE_N + DVE_DS)
                if not first(j):
                    wait(pool, pe_tile, j * PE_N + (PE_SN - PE_N))
                for h in range(2):
                    ins = pool.tensor_tensor(
                        uve[0:64, h, :].rearrange("p (s v) -> p s v", s=NS),
                        uvs[0:64, 64 * h:64 * h + 64].rearrange("p (o v) -> p o v", o=1).to_broadcast([64, NS, 64]),
                        const[0:64, C_SEQ:C_SEQ + NS].rearrange("p (s o) -> p s o", o=1).to_broadcast([64, NS, 64]), ALU.mult)
                ins.then_inc(e_uve, 1)
            wait(pool, stored, 32)
            for v in ew_buf:
                pool.memset(v[2][:, :], 0.0).then_inc(padded, 1)
            elementwise(0, 0)
            tile(0, 0)
            tile(1, 1)
            with pool.Fori(1, RT // 2 - 1) as i:
                ch.enter(i - 1, 2 * EW_MARKS)
                for u in range(2):
                    tile(i * 2 + u, u)
            ch.leave(RT // 2 - 2)
            tile(RT - 2, 0)
            tile(RT - 1, 1, False)
            for j in range(RT):
                wait(pool, gn_var, j + 1)
                pool.tensor_tensor(hT[:, j, :], hT[:, j, :], nrm[:, j % 2, :], ALU.subtract).then_inc(gn_cen, 1)
                wait(pool, gn_nrm, j + 1)
                ch.link(pool.tensor_tensor(hT[:, j, :], hT[:, j, :], z[:, 16 + j, :], ALU.add))
                pool.tensor_tensor(hT[:, j, :], hT[:, j, :], hT[:, 8 + j, :], ALU.mult).then_inc(gn_ready, 1)
            for k in range(KT):
                pool.tensor_scalar(xT[:, k, :], xT[:, k, :], ALPHA, None, ALU.mult).then_inc(xa_ready, 1)

            def load_keys(q):
                with pool.Fori(0, NPAGES) as g:
                    page = pool.value_load(page_ids[0:1, bass.ds(g + q * NPAGES, 1)], min_val=0, max_val=a["cache_krope"].shape[1] - 1)
                    pool.dma_start(kr_pages[:, q % 4, bass.ds(g * ROPE, ROPE)],
                                   a["cache_krope"][0][bass.ds(page, 1), :, :].rearrange("o p c -> (o p) c")).then_inc(kr_in[q % 4], 16)
            pool.wait_ge(ids_in, 16)
            pool.wait_ge(ql_ready, 2 * MH)
            for q in range(4):
                load_keys(q)
            pool.wait_ge(pa_ready, 2 * MH)
            pool.wait_ge(ql_ready, 2 * MH)
            pool.wait_ge(qr_ready, MH)
            for r in range(2):
                for q in range(NS):
                    pool.tensor_copy(qs[:, r, q * 32:(q + 1) * 32].rearrange("p (h t) -> p h t", h=MH),
                                     qlT[:, r, :, NP_TOK + TS * q:NP_TOK + TS * (q + 1)])
            for q in range(NS):
                ins = pool.tensor_copy(qrs[0:64, q * 32:(q + 1) * 32].rearrange("p (h t) -> p h t", h=MH),
                                       qrT[0:64, :, NP_TOK + TS * q:NP_TOK + TS * (q + 1)])
            ins.then_inc(qs_ready, 1)
            for q in range(4, NS):
                pool.wait_ge(sa_tr, 4 * 8 - 3 + (q - 4))
                load_keys(q)
            def sum_tiles(r, n):
                pool.wait_ge(x_added, r * 4 * KT + n + 1)
                if n == 0:
                    if r:
                        pool.wait_ge(x_acc1, KT)
                    pool.tensor_copy(lnb[:, 0, :], xT[:, 0, :]).then_inc(x_acc1, 1)
                else:
                    pool.wait_ge(x_acc1, r * KT + n)
                    pool.tensor_tensor(lnb[:, 0, :], lnb[:, 0, :], xT[:, n, :], ALU.add).then_inc(x_acc1, 1)
            for n in range(KT):
                sum_tiles(0, n)

            def centre(base):
                pool.wait_ge(ln_rstd, base // KT + 1)
                for k in range(KT):
                    pool.tensor_tensor(xT[:, k, :], xT[:, k, :], lnb[:, 2, :], ALU.subtract).then_inc(ln_cen, 1)
            centre(0)
            for k in range(KT):
                pool.wait_ge(h2_ready, k + 1)
                pool.tensor_scalar(xT[:, k, :], xT[:, k, :], ALPHA, None, ALU.mult).then_inc(xa2_ready, 1)
            def square(q, m):
                wait(pool, up_relu, q * KT + (m + 1))
                if not (first(q) and m < 2):
                    wait(pool, f_split, q * KT + (m - 1))
                pool.tensor_tensor(relu_sq[:, m % 2, :], relu[:, m % 2, :], relu[:, m % 2, :], ALU.mult).then_inc(up_f, 1)
            for m in range(KT):
                square(0, m)
            with pool.Fori(1, 4) as q:
                for m in range(KT):
                    square(q, m)
            for n in range(KT):
                sum_tiles(1, n)
            centre(KT)
        @block.scalar
        def _(act):
            ch = Chain(act, act_step)
            act.dma_start(const[:, :], a["const"]).then_inc(const_in, 16)
            act.dma_start(crow[0:1, 0, :], a["c_prompt"]).then_inc(c_in, 16)
            act.dma_start(crow[1:9, 0, :], a["c_sample"]).then_inc(c_in, 16)
            for q in range(2):
                act.dma_start(xrow[:, q, :], a["x_prompt"][0, q * P:(q + 1) * P, :]).then_inc(x_in, 16)
            act.dma_start(xrow[0:32, 2, :], a["x_sample"].rearrange("b t d -> (b t) d")).then_inc(x_in, 16)
            act.dma_start(shrow[0:NS, :], a["state_shift"][0]).then_inc(shift_in, 16)
            act.dma_start(page_ids[0:1, :], a["page_table"].rearrange("s g -> (s g)").rearrange("(o n) -> o n", o=1)).then_inc(ids_in, 16)
            act.wait_ge(padded, 1)

            def param(t, r, src, n, w=P):
                act.dma_start(prow[r:r + n, t, 0:w], src.rearrange("(n w) -> n w", w=w)).then_inc(par_in, 16)
            param(0, 0, a["b_ada"][0], 96)
            param(0, 96, a["rwkv_mu"][0, 0:3 * RW], 24)
            for n, name in enumerate(("rwkv_w0", "rwkv_a0", "rwkv_k_k", "rwkv_k_a")):
                param(1, 8 * n, a[name][0], 8)
            param(1, 32, a["rwkv_r_k"][0].rearrange("h k -> (h k)"), 8)
            for n, name in enumerate(("rwkv_lnx_g", "rwkv_lnx_b", "mla_out_norm")):
                param(1, 40 + 8 * n, a[name][0], 8)
            for n, name in enumerate(("ln1_g", "ln1_b", "ln2_g", "ln2_b")):
                param(1, 64 + 16 * n, a[name][0], 16)
            param(2, 0, a["mla_q_norm"][0], 4)
            param(2, 4, a["mla_kv_norm"][0], 2)
            param(2, 6, a["rwkv_mu"][0, 3 * RW:3 * RW + LORA], 1, LORA)
            param(2, 7, a["rwkv_mu"][0, 3 * RW + LORA:3 * RW + 2 * LORA], 1, LORA)
            param(2, 8, a["rwkv_mu"][0, 3 * RW + 2 * LORA:N_SHIFT], 2)
            act.wait_ge(c_in, 32)
            act.activation(crow[0:9, 1, :], crow[0:9, 0, :], ACT.Sigmoid).then_inc(c_sig, 1)
            act.wait_ge(par_turned, 1)
            act.activation(par[:, 0:256], bank[1][:, 0:256], ACT.Copy)
            act.activation(par[:, 256:272], bank[1][:, 256:272], ACT.Copy).then_inc(par_ready, 1)

            def ada_copy(i, u):
                act.wait_ge(ada_mm, i * RING + (u + 1))
                if not (isinstance(i, int) and i == 0):
                    act.wait_ge(ada_sum, i * RING + (u + 1 - RING))
                act.activation(part[:, u, :], bank[u][:, 0:SLAB_COLS], ACT.Copy).then_inc(ada_part, 1)
            for u in range(RING):
                ada_copy(0, u)
            with act.Fori(1, N_ADA // RING) as i:
                for u in range(RING):
                    ada_copy(i, u)

            def win_copy(mt, b, par_, col, w, wait_free=True):
                act.wait_ge(win_mm, mt + 1)
                if wait_free:
                    act.wait_ge(z_ready, mt - 1)
                    act.wait_ge(last_ready, mt - 1)
                act.activation(pad[0:w, par_, 1:1 + NP_TOK], bank[b][0:w, 0:NP_TOK], ACT.Copy)
                five = pad[0:w, par_, 1 + NP_TOK:1 + NP_TOK + 5 * NS].rearrange("p (s t) -> p s t", t=5)
                act.activation(five[:, :, 0:1], shT[0:w, bass.ds(col, 1), :].rearrange("p o s -> p s o"), ACT.Copy)
                act.activation(five[:, :, 1:5], bank[b][0:w, NP_TOK:NTOK].rearrange("p (s t) -> p s t", t=TS),
                               ACT.Copy).then_inc(win_copied, 1)
            act.wait_ge(sh_ready, 1)
            for mt, (col, w) in enumerate([(24, LORA), (25, LORA), (26, P), (27, P)]):
                win_copy(mt, mt % 4, mt % 2, col, w, mt > 1)
            with act.Fori(0, 3) as i:
                for m in range(8):
                    win_copy(i * 8 + (4 + m), m % 4, m % 2, i * 8 + m, P)
            for mt in range(28, NWIN):
                act.wait_ge(win_mm, mt + 1)
                w = P if mt < 34 else ROPE
                act.activation(mla[0:w, mt - 28, :], bank[mt % 4][0:w, 0:NTOK], ACT.Copy).then_inc(win_copied, 1)
            act.wait_ge(z_ready, 4)
            act.activation(zl[0:LORA, 0, :], zl[0:LORA, 0, :], ACT.Tanh).then_inc(lora_turned, 1)
            act.activation(zl[:, 2:4, :], zl[:, 2:4, :], ACT.Sigmoid).then_inc(lora_turned, 1)
            for j in range(RT):
                act.wait_ge(lora_mm, 2 * j + 1)
                act.activation(sigw[:, j, :], bank[j % 2][:, 0:NTOK], ACT.Sigmoid, bias=par[:, P + j:P + j + 1]).then_inc(lora_sig, 1)
                act.activation(ag[:, j, :], bank[2 + j % 2][:, 0:NTOK], ACT.Sigmoid, bias=par[:, P + 8 + j:P + 9 + j]).then_inc(lora_sig, 1)
            act.wait_ge(stored, 32)
            for j in range(RT):
                if j >= 2:
                    act.wait_ge(kk_mm, j - 1)
                act.activation(sq[:, j % 2, :], z[:, 8 + j, :], ACT.Square, scale=par[:, P + 16 + j:P + 17 + j]).then_inc(kk_sq, 1)
                act.wait_ge(kk_mm, j + 1)
                if j >= 2:
                    act.wait_ge(kk_ready, j - 1)
                act.activation(nrm[:, j % 2, :], bank[6 + j % 2][:, 0:NTOK], ACT.Sqrt).then_inc(kk_nrm, 1)

            def elementwise(j, u):
                abr, bk, rv, pend = ew_buf[u]
                act.wait_ge(ew_scan, j + 1)
                if not first(j):
                    act.wait_ge(ew_pool, j)
                    act.wait_ge(ew_a, j)
                act.activation(dec[:, 0, :], lam, ACT.Exp, scale=-DECAY_C)
                act.activation(dec[:, 1, :], lam, ACT.Exp, scale=DECAY_C)
                act.wait_ge(ew_lp, j + 1)
                act.activation(dec[:, 2, :], sigw[:, bass.ds(j, 1), :].rearrange("p o n -> p (o n)"), ACT.Exp, scale=-DECAY_C
                               ).then_inc(ew_exp, 1)
                if not (isinstance(j, int) and j < 2):
                    act.wait_ge(pe_tile, j * PE_N + (PE_O - 2 * PE_N))
                else:
                    act.wait_ge(padded, 5)
                v = z[:, bass.ds(j + 16, 1), :].rearrange("p o n -> p (o n)")
                act.activation(rv[:, 0:NCH * P].rearrange("p (c n) -> p c n", c=NCH)[:, :, CH:P],
                               v[:, 0:NP_TOK].rearrange("p (c t) -> p c t", c=NCH), ACT.Copy)
                act.activation(rv[:, NCH * P + 32:NCH * P + 64], v[:, NP_TOK:NTOK], ACT.Copy).then_inc(ew_v, 1)

            def tile(j, u, ahead=True):
                act.wait_ge(pe_tile, j * PE_N + PE_A4)
                if not first(j):
                    act.wait_ge(e_nt, j * 5)
                for h in range(2):
                    ins = act.activation(a4[:, 4 * h:4 * h + 4, :], bank[4 + h][:, :].rearrange("p (c t) -> p c t", c=4), ACT.Copy)
                ins.then_inc(act_tile, 1)
                act.wait_ge(pe_tile, j * PE_N + PE_BK)
                act.activation(bkT, bank[0][:, :].rearrange("p (c t) -> p c t", c=4), ACT.Copy).then_inc(act_tile, 1)
                act.wait_ge(pe_tile, j * PE_N + PE_SMP)
                act.activation(bks[0:64, :], bank[7][0:64, 0:P], ACT.Copy).then_inc(act_tile, 1)
                for n in range(5):
                    act.wait_ge(p_y, j * 5 + (n + 1))
                    act.activation(y_sb, bank[6][:, :].rearrange("p (c t) -> p c t", c=4), ACT.Copy).then_inc(e_y, 1)
                    if n == 0:
                        act.wait_ge(pe_tile, j * PE_N + PE_S0)
                        act.activation(s0t, bank[0][:, :].rearrange("p (c t) -> p c t", c=4), ACT.Copy).then_inc(act_tile, 1)
                    if n == 1:
                        act.wait_ge(pe_tile, j * PE_N + PE_YS)
                        act.activation(ts_y[0:32], bank[7][0:32, 0:64].rearrange("p (h c) -> p h c", h=2), ACT.Copy).then_inc(act_tile, 1)
                    if n == 4:
                        act.wait_ge(pe_tile, j * PE_N + PE_US)
                        act.activation(uvs[0:32, :], bank[7][0:32, 256:384], ACT.Copy).then_inc(act_tile, 1)
                if ahead:
                    elementwise(j + 1, 1 - u)
                for c in range(NCH):
                    r = CH * (c % 2)
                    act.wait_ge(p_d, j * NCH + (c + 1))
                    act.activation(d_sb[r:r + CH, 0:HD], bank[0][r:r + CH, 0:HD], ACT.Copy)
                    act.activation(d_sb[r:r + CH, HD:P], bank[1][r:r + CH, 0:HD], ACT.Copy).then_inc(e_d, 1)
                    act.wait_ge(ada_mm, j * 4 + (N_ADA + c + 1))
                    act.wait_ge(ada_sum, j * 4 + (N_ADA + c - 3))
                    act.activation(part[:, c, :], bank[4 + c % 2][:, 0:SLAB_COLS], ACT.Copy).then_inc(ada_part, 1)
                act.wait_ge(pe_tile, j * PE_N + PE_O)
                act.activation(hT[:, bass.ds(j, 1), :].rearrange("p o n -> p (o n)"), bank[3][:, 0:NTOK], ACT.Copy).then_inc(act_tile, 1)
                act.wait_ge(pe_tile, j * PE_N + PE_SNT)
                if not first(j):
                    act.wait_ge(state_out, j * (16 * 9))
                act.activation(s1n, bank[4][:, :].rearrange("p (c t) -> p c t", c=4), ACT.Copy).then_inc(act_tile, 1)
                act.wait_ge(pe_tile, j * PE_N + PE_STT)
                act.activation(sto[0:64, :], bank[5][0:64, 0:P], ACT.Copy).then_inc(act_tile, 1)
            elementwise(0, 0)
            tile(0, 0)
            tile(1, 1)
            with act.Fori(1, RT // 2 - 1) as i:
                for u in range(2):
                    tile(i * 2 + u, u)
            tile(RT - 2, 0)
            tile(RT - 1, 1, False)
            for j in range(RT):
                if j >= 2:
                    act.wait_ge(gn_mm, j - 1)
                act.activation(sq[:, j % 2, :], hT[:, j, :], ACT.Square).then_inc(gn_sq, 1)
                act.wait_ge(gn_var, j + 1)
                act.activation(gnv[:, j % 2, :], gnv[:, j % 2, :], ACT.Sqrt, bias=eps[:, 0:1]).then_inc(gn_std, 1)
            act.activation(sqm, mla[:, 0:6, :], ACT.Square).then_inc(m_sq, 1)
            for n, dim in enumerate((QR, KVR)):
                act.wait_ge(m_mm, n + 1)
                act.activation(rin[:, n, :], bank[4 + n][:, 0:NTOK], ACT.Sqrt, scale=1.0 / dim, bias=eps[:, 1:2]).then_inc(m_std, 1)
            for n in range(4):
                act.wait_ge(uk_turned, n + 1)
                act.activation(ukT[:, 2 * n:2 * n + 2, :], bank[n][:, :].rearrange("p (h r) -> p h r", h=2), ACT.Copy).then_inc(uk_ready, 1)
            for h in range(MH):
                act.wait_ge(q_mm, h + 1)
                if h >= 2:
                    act.wait_ge(ql_mm, h - 1)
                    act.wait_ge(qr_ready, h - 1)
                act.activation(qn[:, h % 2, :], bank[h % 2][:, 0:NTOK], ACT.Copy)
                act.activation(qraw[0:64, h % 2, :], bank[2 + h % 2][0:64, 0:NTOK], ACT.Copy).then_inc(q_copied, 1)
                act.wait_ge(ql_mm, h + 1)
                for r in range(2):
                    act.activation(qlT[:, r, h, :], bank[6 + r][:, 0:NTOK], ACT.Copy).then_inc(ql_ready, 1)
            act.wait_ge(lat_turned, 1)
            act.wait_ge(gn_ready, RT)
            for t, rows in enumerate((P, P, 32)):
                act.activation(latN[0:rows, t, :], bank[t][0:rows, 0:KVR], ACT.Copy).then_inc(lat_rows, 1)
            act.activation(krN[:, 0:128], bank[3][:, 0:128], ACT.Copy)
            act.activation(krN[0:32, 128:192], bank[3][0:32, 128:192], ACT.Copy).then_inc(lat_rows, 1)
            for n in range(2 * MH):
                nk = (n % 2 + 1) * P
                act.wait_ge(pa_max, n + 1)
                act.activation(S2[:, n % 2, 0:nk], S2[:, n % 2, 0:nk], ACT.Exp, scale=SM_SCALE, bias=sm[:, n % 2:n % 2 + 1],
                               accum_out=sm[:, 2 + n % 2:3 + n % 2]).then_inc(pa_exp, 1)
                act.wait_ge(pa_T, n + 1)
                if n >= 2:
                    act.wait_ge(pa_ctx, n - 1)
                act.activation(pT2[:, n % 2, 0:nk], bank[6][:, 0:nk], ACT.Copy).then_inc(pa_pT, 1)
            for g in range(2):
                for kb in range(8):
                    for q in range(4):
                        act.wait_ge(sa_tr, (g * 8 + kb) * 4 + q + 1)
                        if g or kb:
                            act.wait_ge(sa_s, g * 9 + kb)
                        if q < 3:
                            act.activation(latS[:, q, :], bank[q][:, :], ACT.Copy).then_inc(sa_lat, 1)
                act.wait_ge(sa_max, g + 1)
                act.activation(S, S, ACT.Exp, scale=SM_SCALE, bias=sm[:, 4:5], accum_out=sm[:, 5:6]).then_inc(sa_exp, 1)
                for b in (0, 2, 4):
                    act.wait_ge(sa_T, g * 5 + b + 1)
                    if b < 4:
                        act.activation(pT[:, 4 * b:4 * b + 4, :], bank[b][:, :].rearrange("p (k q) -> p k q", k=4), ACT.Copy).then_inc(sa_pT, 1)
                    else:
                        act.activation(pT[0:32, 16, :], bank[4][0:32, 0:P], ACT.Copy).then_inc(sa_pT, 1)
                act.wait_ge(sa_ctx, g + 1)
                act.wait_ge(sa_rinv, g + 1)
                act.activation(ctxs, bank[6][:, 0:KVR], ACT.Copy, scale=sm[:, 6:7]).then_inc(sa_ctx_n, 1)
            act.wait_ge(stored, 16 * 8)
            for h in range(MH):
                act.wait_ge(om_mm, h + 1)
                act.activation(hT[:, 8 + h, :], bank[h % 2][:, 0:NTOK], ACT.Copy)
                if h >= 2:
                    act.wait_ge(om_sum, h - 1)
                act.activation(osq[:, h % 2, :], bank[h % 2][:, 0:NTOK], ACT.Square).then_inc(om_sq, 1)
            act.wait_ge(om_sum, MH)
            act.activation(lnb[:, 3, :], bank[2][:, 0:NTOK], ACT.Sqrt, scale=1.0 / RW, bias=eps[:, 1:2]).then_inc(om_std, 1)

            def squares(r, n):
                act.wait_ge(x_added, r * 4 * KT + n + 1)
                if n >= 2 or r:
                    act.wait_ge(x_acc2, r * KT + n - 1)
                act.activation(lnb[:, 4 + n % 2, :], xT[:, n, :], ACT.Square).then_inc(x_sq, 1)
            for n in range(KT):
                squares(0, n)

            def norm(r, gcol):
                act.wait_ge(ln_var, r + 1)
                act.activation(lnb[:, 3, :], lnb[:, 3, :], ACT.Sqrt, bias=eps[:, 2:3]).then_inc(ln_std, 1)
                for k in range(KT):
                    act.wait_ge(ln_nrm, r * KT + k + 1)
                    act.activation(xT[:, k, :], xT[:, k, :], ACT.Identity, scale=par[:, gcol + k:gcol + k + 1],
                                   bias=par[:, gcol + KT + k:gcol + KT + k + 1]).then_inc(ln_x, 1)
            norm(0, P + 64)
            def up_copy(q, m):
                act.wait_ge(tile_mm, q * 2 * KT + (KT + m + 1))
                if not (first(q) and m < 2):
                    act.wait_ge(up_f, q * KT + (m - 1))
                act.activation(relu[:, m % 2, :], bank[m % 4][:, 0:NTOK], ACT.Relu).then_inc(up_relu, 1)
            for m in range(KT):
                up_copy(0, m)
            with act.Fori(1, 4) as q:
                for m in range(KT):
                    up_copy(q, m)
            for n in range(KT):
                squares(1, n)
            norm(1, P + 96)
            for n in range(1, 12, 2):
                q = n % 3
                rows = P if q < 2 else 32
                act.wait_ge(y_T, n + 1)
                act.activation(y_rows[0:rows, q, (n // 3) * 512:(n // 3 + 1) * 512], bank[n % 4][0:rows, :], ACT.Copy).then_inc(y_rows_a, 1)
        @block.tensor
        def _(pe):
            pe.wait_ge(const_in, 16)
            pe.wait_ge(c_silu, 1)
            for k in range(KT):
                t = pe.transpose(bank[0][:, 9 * k:9 * k + 9], crow[0:9, 2, k * P:(k + 1) * P], ident[0:9, 0:9])
            t.then_inc(c_turned, 1)
            pe.wait_ge(par_in, 16 * 19)
            for t in range(2):
                pe.transpose(bank[1][:, t * P:(t + 1) * P], prow[:, t, :], ident)
            pe.transpose(bank[1][:, 256:272], prow[0:16, 2, :], ident[0:16, 0:16]).then_inc(par_turned, 1)
            pe.wait_ge(shift_in, 16)
            for t in range(24):
                pe.transpose(bank[2][:, NS * t:NS * t + NS], shrow[0:NS, t * P:(t + 1) * P], ident[0:NS, 0:NS])
            for t, (c0, w) in enumerate([(3 * RW, LORA), (3 * RW + LORA, LORA), (3 * RW + 2 * LORA, P), (3 * RW + 2 * LORA + P, P)]):
                c = NS * (24 + t)
                tr = pe.transpose(bank[2][0:w, c:c + NS], shrow[0:NS, c0:c0 + w], ident[0:NS, 0:NS])
            tr.then_inc(sh_turned, 1)
            pe.wait_ge(x_in, 48)
            for k in range(KT):
                if k >= 4:
                    pe.wait_ge(x_ready, k - 3)
                b = bank[4 + k % 4]
                for q in range(2):
                    pe.transpose(b[:, q * P:(q + 1) * P], xrow[:, q, k * P:(k + 1) * P], ident)
                pe.transpose(b[:, 256:288], xrow[0:32, 2, k * P:(k + 1) * P], ident[0:32, 0:32]).then_inc(x_turned, 1)

            pe.wait_ge(c_ready, 1)
            pe.wait_ge(par_ready, 1)
            pe.wait_ge(sh_ready, 1)
            pe.wait_ge(x_ready, 16)

            def ada_columns(b, weights, ks):
                for k in ks:
                    g = 32 * (k % 4)
                    mm = pe.matmul(b[g:g + 32, 0:SLAB_COLS], cT[:, 9 * k:9 * k + 32], weights[:, k, :],
                                   start=(k < 4), stop=(k >= KT - 4))
                return mm

            def ada_product(i, u):
                pe.wait_ge(slab_in[u], i * 16 + 16)
                if not (isinstance(i, int) and i == 0):
                    pe.wait_ge(ada_part, i * RING + (u + 1 - RING))
                ada_columns(bank[u], slab[u], range(KT)).then_inc(ada_mm, 1)

            def ada_turn(i, u):
                pe.wait_ge(ada_part, i * RING + (u + 1))
                if not (isinstance(i, int) and i == 0 and u < 2):
                    pe.wait_ge(mod_ready, i * RING + (u - 1))
                for m in range(2):
                    mm = pe.matmul(bank[4 + u % 2][:, 9 * m:9 * m + 9], part[:, u, m * P:(m + 1) * P],
                                   const[:, C_SEL:C_SEL + 9], start=True, stop=True)
                mm.then_inc(ada_sum, 1)

            def ada_four(i):
                for u in range(RING):
                    ada_product(i, u)
                    if u:
                        ada_turn(i, u - 1)
                ada_turn(i, RING - 1)
            ada_four(0)
            with pe.Fori(1, N_ADA // RING) as i:
                ada_four(i)

            def column_tile(b, s, c0, w, first_wait=None):
                for k in range(KT):
                    if first_wait:
                        pe.wait_ge(h_ready, k + 1)
                    mm = pe.matmul(bank[b][0:w, 0:NTOK], slab[s][:, k, c0:c0 + w], hT[:, k, :],
                                   start=(k == 0), stop=(k == KT - 1))
                return mm

            pe.wait_ge(ada_part, N_ADA)

            def win_tile(mt, s, c0, w, b, first=False):
                if not first:
                    pe.wait_ge(win_copied, mt - 3)
                column_tile(b, s, c0, w, isinstance(mt, int) and mt == 0).then_inc(win_mm, 1)
            for mt, w in enumerate((LORA, LORA, P, P)):
                n = WIN0 + mt // 2
                pe.wait_ge(slab_in[n % RING], slab_ready(n))
                win_tile(mt, n % RING, (mt % 2) * w, w, mt, True)
            with pe.Fori(0, N_RKV // RING) as i:
                for m in range(2 * RING):
                    s = (WIN0 + 2 + m // 2) % RING
                    pe.wait_ge(slab_in[s], i * 16 + slab_ready(WIN0 + 2 + m // 2))
                    win_tile(i * 2 * RING + (4 + m), s, (m % 2) * P, P, m % 4)
            for mt in range(28, NWIN):
                n = WIN0 + mt // 2
                pe.wait_ge(slab_in[n % RING], slab_ready(n))
                win_tile(mt, n % RING, (mt % 2) * P, P if mt < 34 else ROPE, mt % 4)
            pe.wait_ge(last_ready, 28)
            for c in range(4):
                pe.wait_ge(win_copied, min(NWIN, 32 + c))
            for t in range(28):
                if t >= 16 and t % 4 == 0:
                    pe.wait_ge(last_out, t // 4 - 3)
                w = LORA if t in (24, 25) else P
                tr = pe.transpose(bank[(t // 4) % 4][0:9, (t % 4) * P:(t % 4) * P + w], last[0:w, t, :], ident[0:w, 0:w])
                if t % 4 == 3:
                    tr.then_inc(last_turned, 1)
            wait(pe, lora_turned, 2)
            wait(pe, slab_in[LOR % RING], slab_ready(LOR))
            wait(pe, win_copied, NWIN)
            wait(pe, last_out, 7)
            for j in range(RT):
                if j >= 2:
                    wait(pe, lora_sig, 2 * j - 2)
                    wait(pe, g_ready, j - 1)
                cols = slice(j * P, (j + 1) * P)
                pe.matmul(bank[j % 2][:, 0:NTOK], w2_v[:, cols], zl[0:LORA, 0, :], start=True, stop=True)
                pe.matmul(bank[2 + j % 2][:, 0:NTOK], a2_v[:, cols], zl[0:LORA, 1, :], start=True, stop=True).then_inc(lora_mm, 1)
                for k in range(2):
                    mm = pe.matmul(bank[4 + j % 2][:, 0:NTOK], g2_v[:, k, cols], zl[:, 2 + k, :], start=(k == 0), stop=(k == 1))
                mm.then_inc(lora_mm, 1)
            for j in range(RT):
                wait(pe, kk_sq, j + 1)
                if j >= 2:
                    wait(pe, kk_nrm, j - 1)
                pe.matmul(bank[6 + j % 2][:, 0:NTOK], blk, sq[:, j % 2, :], start=True, stop=True).then_inc(kk_mm, 1)
            wait(pe, lora_sig, 2 * RT)
            wait(pe, g_ready, RT)
            wait(pe, kk_nrm, RT)

            def late_product(j, c, ks):
                s = LATE_SLOTS[c % 2]
                if ks[0] == 0:
                    wait(pe, slab_in[s], j * 32 + (slab_ready(QUP + c % 2 - RING) + 16 * (c // 2 + 1)))
                    wait(pe, mod_ready, j * 4 + (N_ADA + c - 1))
                return ada_columns(bank[4 + c % 2], slab[s], ks)

            def late_turn(j, c):
                wait(pe, ada_part, j * 4 + (N_ADA + c + 1))
                for m in range(2):
                    mm = pe.matmul(bank[4 + c % 2][:, 256 + 9 * m:265 + 9 * m], part[:, c, m * P:(m + 1) * P],
                                   const[:, C_SEL:C_SEL + 9], start=True, stop=True)
                mm.then_inc(ada_sum, 1)

            def tile(j, u):
                abr, bk, rv, pend = ew_buf[u]
                H = [slice(64 * h, 64 * h + 64) for h in range(2)]
                wait(pe, ew_pool, j + 1)
                wait(pe, ew_v, j + 1)
                wait(pe, ew_a, j + 1)
                if not first(j):
                    wait(pe, act_tile, j * ACT_N + (ACT_O - ACT_N))
                    wait(pe, act_tile, j * ACT_N + (ACT_SNT - ACT_N))
                    wait(pe, act_tile, j * ACT_N + (ACT_STT - ACT_N))
                for q in range(2):
                    tok = slice(q * P, (q + 1) * P)
                    for h in range(2):
                        pe.matmul(bank[4 + h][:, q * P:(q + 1) * P], abr[H[h], 0, tok], abr[H[h], 1, tok], start=True, stop=True)
                    for h in range(2):
                        mm = pe.matmul(bank[4 + h][:, (2 + q) * P:(3 + q) * P], abr[H[h], 1, tok], abr[H[h], 0, tok], start=True, stop=True)
                mm.then_inc(pe_tile, 1)
                for c in range(NCH):
                    tr = pe.transpose(bank[0][:, c * P:(c + 1) * P], bk[:, c * P:(c + 1) * P], ident)
                tr.then_inc(pe_tile, 1)
                for c in range(NCH):
                    tr = pe.transpose(bank[1][:, c * P:(c + 1) * P], rv[:, c * P:(c + 1) * P], ident)
                tr.then_inc(pe_tile, 1)
                pe.transpose(bank[7][0:64, 0:P], bk[:, NCH * P:NCH * P + 64], ident)
                pe.transpose(bank[7][0:64, P:2 * P], rv[:, NCH * P:NCH * P + 64], ident)
                for h in range(2):
                    pe.matmul(bank[7 - h][0:64, 256:320], bk[H[h], NCH * P:NCH * P + 64],
                              abr[H[h], 0:3:2, NP_TOK:NTOK], start=True, stop=True)
                for h in range(2):
                    mm = pe.matmul(bank[7 - h][0:32, 320:352], abr[H[h], 0, NP_TOK:NTOK],
                                   abr[H[h], 1, NP_TOK:NTOK], start=True, stop=True)
                mm.then_inc(pe_tile, 1)
                for h in range(2):
                    for c in range(NCH):
                        mm = pe.matmul(bank[2 + h][:, c * P:(c + 1) * P], bk[H[h], c * P:(c + 1) * P],
                                       abr[H[h], 0:3:2, c * CH:(c + 1) * CH], start=True, stop=True)
                mm.then_inc(pe_tile, 1)

                def between(n):
                    if n == 0:
                        wait(pe, act_tile, j * ACT_N + ACT_BK)
                        wait(pe, s0_in, j * 128 + 128)
                        for q in range(4):
                            tr = pe.transpose(bank[0][:, q * P:(q + 1) * P], s0n[:, q, :], ident)
                        tr.then_inc(pe_tile, 1)
                        wait(pe, dve_tile, j * DVE_N + DVE_RV)
                        wait(pe, ew_rk, j + 1)
                        pe.matmul(bank[1][:, 0:NTOK], blk, rkk, start=True, stop=True).then_inc(pe_tile, 1)
                    if n == 1:
                        wait(pe, dve_tile, j * DVE_N + DVE_NTS)
                        wait(pe, act_tile, j * ACT_N + ACT_SMP)
                        for h in range(2):
                            mm = pe.matmul(bank[7][0:32, 32 * h:32 * h + 32], ts_n[0:32, h, :], ts_m[0:32, h, :], start=True, stop=True)
                        mm.then_inc(pe_tile, 1)
                        wait(pe, act_tile, j * ACT_N + ACT_S0)
                        wait(pe, dve_tile, j * DVE_N + DVE_AR)
                        for h in range(2):
                            mm = pe.matmul(bank[2 + h][0:64, :], arS[u][H[h], :], s0t[H[h], :, :], start=True, stop=True)
                        mm.then_inc(pe_tile, 1)
                    if n == 2:
                        wait(pe, act_tile, j * ACT_N + ACT_YS)
                        for h in range(2):
                            mm = pe.matmul(bank[7][0:32, 64 + 32 * h:96 + 32 * h], ts_y[0:32, h, :], ts_t[0:32, h, :], start=True, stop=True)
                        mm.then_inc(pe_tile, 1)
                        wait(pe, dve_tile, j * DVE_N + DVE_TS)
                        for h in range(2):
                            mm = pe.matmul(bank[7][0:32, P + 64 * h:P + 64 * h + 64], ars[32:64, h, 0:32], uvs[32:64, H[h]], start=True, stop=True)
                        mm.then_inc(pe_tile, 1)
                    if n == 3:
                        wait(pe, dve_tile, j * DVE_N + DVE_XS)
                        for h in range(2):
                            mm = pe.matmul(bank[7][0:32, 256 + 64 * h:320 + 64 * h], ts_t[0:32, h, :], d_smp[0:32, H[h]], start=True, stop=True)
                        mm.then_inc(pe_tile, 1)
                    if n == 4:
                        wait(pe, act_tile, j * ACT_N + ACT_US)
                        for h in range(2):
                            mm = pe.matmul(bank[7][32:64, 384 + 64 * h:448 + 64 * h], ars[0:64, h, 32:64], uvs[0:64, H[h]], start=True, stop=True)
                        mm.then_inc(pe_tile, 1)
                for n in range(5):
                    wait(pe, e_nt, j * 5 + (n + 1))
                    wait(pe, e_t, j * 6 + (n + 1))
                    if n == 0:
                        wait(pe, dve_tile, j * DVE_N + DVE_NTS)
                        if not first(j):
                            wait(pe, dve_tile, j * DVE_N + (DVE_SN - DVE_N))
                    for c in range(4):
                        mm = pe.matmul(bank[6][:, c * P:(c + 1) * P], nt_v[n % 2][:, c, :], tm[:, c, :], start=True, stop=True)
                    mm.then_inc(p_y, 1)
                    between(n)
                    wait(pe, e_y, j * 5 + (n + 1))
                    if n < 4:
                        for c in range(4):
                            pe.matmul(bank[4][:, c * P:(c + 1) * P], tt[:, c, :], y_sb[:, c, :], start=True, stop=True)
                    for c in range(4):
                        mm = pe.matmul(bank[5][:, c * P:(c + 1) * P], y_sb[:, c, :], tt[:, c, :], start=True, stop=True)
                    mm.then_inc(p_inc, 1)
                wait(pe, e_t, j * 6 + 6)
                wait(pe, dve_tile, j * DVE_N + DVE_DS)
                wait(pe, dve_tile, j * DVE_N + DVE_BON)
                wait(pe, dve_tile, j * DVE_N + DVE_OS)
                for c in range(NCH):
                    r = slice(CH * (c % 2), CH * (c % 2) + CH)
                    tok = slice(c * CH, (c + 1) * CH)
                    if c:
                        wait(pe, e_st, j * NCH + c)
                    for h in range(2):
                        mm = pe.matmul(bank[h][r, 0:HD], ar[64:128, h * NCH + c, 0:CH], uv[64:128, c, H[h]], start=True, stop=(c == 0))
                    if c:
                        mm.then_inc(p_x, 1)
                        wait(pe, p_x, j * (NCH - 1) + c)
                        for h in range(2):
                            mm = pe.matmul(bank[h][r, 0:HD], abr[H[h], 0, tok], st[H[h], (c - 1) % 2, :], start=False, stop=True)
                    mm.then_inc(p_d, 1)
                    late_product(j, c, range(0, 8))
                    wait(pe, e_d, j * NCH + (c + 1))
                    for h in range(2):
                        mm = pe.matmul(bank[7][0:64, H[h]], tt[r, 2 * h + c // 2, r], d_sb[r, H[h]], start=True, stop=True)
                    mm.then_inc(p_u, 1)
                    late_product(j, c, range(8, KT)).then_inc(ada_mm, 1)
                    if c == 0:
                        wait(pe, e_uve, j + 1)
                        for h in range(2):
                            mm = pe.matmul(bank[6][H[h], :], bks[0:64, H[h]], uve[0:64, h, :], start=True, stop=True)
                        mm.then_inc(pe_tile, 1)
                    wait(pe, e_u, j * NCH + (c + 1))
                    for h in range(2):
                        mm = pe.matmul(bank[2][H[h], 0:HD], bkT[:, c, H[h]], uv[:, c, H[h]], start=True, stop=True)
                    mm.then_inc(p_s, 1)
                    for h in range(2):
                        pe.matmul(bank[3][H[h], tok], uv[:, c, H[h]], ar[:, h * NCH + c, CH:P], start=True, stop=(c == 0))
                        if c:
                            pe.matmul(bank[3][H[h], tok], st[H[h], (c - 1) % 2, :], abr[H[h], 2, tok], start=False, stop=True)
                    late_turn(j, c)
                wait(pe, dve_tile, j * DVE_N + DVE_OS)
                pe.transpose(bank[3][:, NP_TOK:NTOK], o_smp[32:64, :], ident[32:64, 32:64]).then_inc(pe_tile, 1)
                wait(pe, dve_tile, j * DVE_N + DVE_SN)
                wait(pe, mod_ready, j * 4 + (N_ADA + 4))
                for q in range(4):
                    tr = pe.transpose(bank[4][:, q * P:(q + 1) * P], s0t[:, q, :], ident)
                tr.then_inc(pe_tile, 1)
                wait(pe, e_st, j * NCH + NCH)
                pe.transpose(bank[5][0:64, 0:P], st[:, (NCH - 1) % 2, :], ident).then_inc(pe_tile, 1)
            pairs(pe, tile)
            pe.wait_ge(act_tile, (RT - 1) * ACT_N + ACT_STT)
            pe.wait_ge(act_tile, (RT - 1) * ACT_N + ACT_SNT)
            for j in range(RT):
                pe.wait_ge(act_tile, (RT - 1) * ACT_N + ACT_O)
                if j >= 2:
                    pe.wait_ge(gn_var, j - 1)
                pe.wait_ge(gn_sq, j + 1)
                pe.matmul(bank[j % 2][:, 0:NTOK], blk, hT[:, j, :], start=True, stop=True)
                pe.matmul(bank[2 + j % 2][:, 0:NTOK], blk, sq[:, j % 2, :], start=True, stop=True).then_inc(gn_mm, 1)
            pe.wait_ge(m_sq, 1)
            for n, (k0, k1) in enumerate(((0, 4), (4, 6))):
                for k in range(k0, k1):
                    mm = pe.matmul(bank[4 + n][:, 0:NTOK], ones, sqm[:, k, :], start=(k == k0), stop=(k == k1 - 1))
                mm.then_inc(m_mm, 1)
            rot = const[0:64, C_ROT:C_ROT + 64]
            pe.matmul(bank[6][0:64, 0:NTOK], rot, mla[0:64, 6, :], start=True, stop=True).then_inc(m_mm, 1)
            pe.wait_ge(slab_in[WUK % RING], slab_ready(WUK))
            pe.wait_ge(gn_var, RT)
            uk = ring[WUK % RING][:, 0:2 * MH * NOPE].rearrange("p (r c) -> p r c", r=2)
            for h in range(MH):
                for r in range(2):
                    tr = pe.transpose(bank[h // 2][:, (h % 2) * KVR + r * P:(h % 2) * KVR + r * P + P], uk[:, r, h * P:(h + 1) * P], ident)
                if h % 2:
                    tr.then_inc(uk_turned, 1)
            pe.wait_ge(m_ready, 4)
            pe.wait_ge(uk_ready, 4)
            pe.wait_ge(kr_ready, 1)
            quv = [slab[(QUP + n) % RING].rearrange("p k c -> p (k c)").rearrange("p (k c) -> p k c", k=4) for n in range(2)]

            def up_project(h):
                n, c = (0, h * QH) if h < 5 else (1, (h - 5) * QH)
                if h in (0, 5):
                    pe.wait_ge(slab_in[(QUP + n) % RING], slab_ready(QUP + n))
                if h >= 2:
                    pe.wait_ge(q_copied, h - 1)
                for k in range(4):
                    pe.matmul(bank[h % 2][:, 0:NTOK], quv[n][:, k, c:c + NOPE], cqn[:, k, :], start=(k == 0), stop=(k == 3))
                for k in range(4):
                    mm = pe.matmul(bank[2 + h % 2][0:64, 0:NTOK], quv[n][:, k, c + NOPE:c + QH], cqn[:, k, :], start=(k == 0), stop=(k == 3))
                mm.then_inc(q_mm, 1)
            up_project(0)
            for h in range(MH):
                if h + 1 < MH:
                    up_project(h + 1)
                pe.wait_ge(q_copied, h + 1)
                if h >= 2:
                    pe.wait_ge(qr_ready, h - 1)
                pe.matmul(bank[4 + h % 2][0:64, 0:NTOK], rot, qraw[0:64, h % 2, :], start=True, stop=True).then_inc(q_rot, 1)
                if h:
                    pe.wait_ge(ql_ready, 2 * h)
                for r in range(2):
                    mm = pe.matmul(bank[6 + r][:, 0:NTOK], ukT[:, h, r * P:(r + 1) * P], qn[:, h % 2, :], start=True, stop=True)
                mm.then_inc(ql_mm, 1)
            pe.wait_ge(m_ready, 6)
            pe.wait_ge(q_copied, MH)
            for t, w in enumerate((P, P, 32)):
                for r in range(2):
                    pe.transpose(bank[t][0:w, r * P:(r + 1) * P], latT[:, r, t * P:t * P + w], ident)
            for t, w in enumerate((P, P, 32)):
                tr = pe.transpose(bank[3][0:w, t * 64:t * 64 + 64], krT[0:64, t * P:t * P + w], ident[0:64, 0:64])
            tr.then_inc(lat_turned, 1)

            def scores(n):
                h, q = n // 2, n % 2
                if n < 2:
                    pe.wait_ge(ql_ready, 2 * MH)
                    pe.wait_ge(qr_ready, MH)
                else:
                    pe.wait_ge(pa_max, n - 1)
                tok, nk = slice(q * P, (q + 1) * P), (q + 1) * P
                b = bank[4 + n % 2][:, 0:nk]
                pe.matmul(b, qrT[0:64, h, tok], krT[0:64, 0:nk], start=True, stop=False)
                pe.matmul(b, qlT[:, 0, h, tok], latT[:, 0, 0:nk], start=False, stop=False)
                pe.matmul(b, qlT[:, 1, h, tok], latT[:, 1, 0:nk], start=False, stop=True).then_inc(pa_s, 1)
            scores(0)
            pe.wait_ge(lat_rows, 4)
            for n in range(2 * MH):
                if n + 1 < 2 * MH:
                    scores(n + 1)
                nb = n % 2 + 1
                pe.wait_ge(pa_p, n + 1)
                if n:
                    pe.wait_ge(pa_pT, n)
                for k in range(nb):
                    tr = pe.transpose(bank[6][:, k * P:(k + 1) * P], S2[:, n % 2, k * P:(k + 1) * P], ident)
                tr.then_inc(pa_T, 1)
                pe.wait_ge(pa_pT, n + 1)
                if n:
                    pe.wait_ge(pa_ready, n)
                for r in range(2):
                    for k in range(nb):
                        mm = pe.matmul(bank[7][:, r * P:(r + 1) * P], latN[:, k, r * P:(r + 1) * P], pT2[:, n % 2, k * P:(k + 1) * P],
                                       start=(k == 0), stop=(k == nb - 1))
                mm.then_inc(pa_ctx, 1)

            def turn_keys(g, kb):
                for q in range(4):
                    s = (CACHE0 + 4 * g + q) % RING
                    if kb == 0:
                        pe.wait_ge(slab_in[s], slab_ready(CACHE0 + 4 * g + q))
                        pe.wait_ge(kr_in[q], 16 * NPAGES * (g + 1))
                    else:
                        m = g * 8 + kb
                        pe.wait_ge(sa_lat, 3 * m)
                        pe.wait_ge(sa_kr, 3 * m + 2 * g)
                    if kb == 0 and g:
                        pe.wait_ge(sa_pT, 3 * g)
                        pe.wait_ge(sa_kr, 3 * 8 * g + 2 * g)
                        pe.wait_ge(sa_ready, g)
                    for r in range(2):
                        for e in range(2):
                            pe.transpose(bank[q][:, r * 256 + e * P:r * 256 + e * P + P], slab[s][:, 2 * kb + e, r * P:(r + 1) * P], ident)
                    for e in range(2):
                        c = (q % 2) * 256 + e * P
                        tr = pe.transpose(bank[4 if q < 2 else 7][0:64, c:c + P], kr_pages[:, q, (2 * kb + e) * ROPE:(2 * kb + e + 1) * ROPE], ident)
                    tr.then_inc(sa_tr, 1)

            def key_scores(g, kb):
                m = g * 8 + kb
                pe.wait_ge(sa_lat, 3 * (m + 1))
                pe.wait_ge(sa_kr, 3 * (m + 1) + 2 * g)
                if kb >= 2 or g:
                    pe.wait_ge(sa_copied, g * 9 + kb - 1)
                b = bank[5 + kb % 2]
                for part_ in range(3):
                    for q in range(4):
                        seq = slice((4 * g + q) * 32, (4 * g + q + 1) * 32)
                        out = b[32 * q:32 * q + 32, 0:256]
                        if part_ < 2:
                            mm = pe.matmul(out, qs[:, part_, seq], latS[:, q, part_ * 256:(part_ + 1) * 256], start=(part_ == 0), stop=False)
                        else:
                            mm = pe.matmul(out, qrs[0:64, seq], krS[0:64, q // 2, (q % 2) * 256:(q % 2 + 1) * 256], start=False, stop=True)
                mm.then_inc(sa_s, 1)
            pe.wait_ge(qs_ready, 1)
            pe.wait_ge(pa_ready, 2 * MH)
            pe.wait_ge(pa_pT, 2 * MH)
            for g in range(2):
                turn_keys(g, 0)
                for kb in range(8):
                    key_scores(g, kb)
                    if kb < 7:
                        turn_keys(g, kb + 1)
                pe.wait_ge(sa_copied, g * 9 + 7)
                for part_ in range(3):
                    for q in range(4):
                        seq = slice((4 * g + q) * 32, (4 * g + q + 1) * 32)
                        out = bank[5][32 * q:32 * q + 32, 0:32]
                        if part_ < 2:
                            mm = pe.matmul(out, qs[:, part_, seq], latT[:, part_, NP_TOK:NTOK], start=(part_ == 0), stop=False)
                        else:
                            mm = pe.matmul(out, qrs[0:64, seq], krT[0:64, NP_TOK:NTOK], start=False, stop=True)
                mm.then_inc(sa_s, 1)
                pe.wait_ge(sa_exp, g + 1)
                for b in range(4):
                    for e in range(4):
                        k = 4 * b + e
                        tr = pe.transpose(bank[b][:, e * P:(e + 1) * P], S[:, k * P:(k + 1) * P], ident)
                    tr.then_inc(sa_T, 1)
                pe.transpose(bank[4][0:32, 0:P], S[:, 2048:2080], ident).then_inc(sa_T, 1)
                pe.wait_ge(sa_pT, 3 * (g + 1))
                pe.wait_ge(sa_kr, 3 * 8 * (g + 1) + 2 * (g + 1))
                pe.wait_ge(sa_copied, 9 * (g + 1))
                for k in range(NPAGES + 1):
                    for q in range(4):
                        s = (CACHE0 + 4 * g + q) % RING
                        out = bank[6][32 * q:32 * q + 32, 0:KVR]
                        if k < NPAGES:
                            mm = pe.matmul(out, pT[:, k, 32 * q:32 * q + 32], slab[s][:, k, :], start=(k == 0), stop=False)
                        else:
                            mm = pe.matmul(out, pT[0:32, k, 32 * q:32 * q + 32], latN[0:32, 2, :], start=False, stop=True)
                mm.then_inc(sa_ctx, 1)
                pe.wait_ge(sa_ctx_n, g + 1)
                for r in range(2):
                    tr = pe.transpose(bank[7][:, r * P:(r + 1) * P], ctxs[:, r * P:(r + 1) * P], ident)
                tr.then_inc(sa_ctxT, 1)
            pe.wait_ge(sa_ready, 2)
            pe.wait_ge(uv_in, 16)

            def value_sum(h):
                pe.wait_ge(om_sq, h + 1)
                pe.matmul(bank[2][:, 0:NTOK], ones, osq[:, h % 2, :], start=(h == 0), stop=(h == MH - 1)).then_inc(om_sum, 1)
            for h in range(MH):
                if h >= 2:
                    pe.wait_ge(om_sq, h - 1)
                for r in range(2):
                    mm = pe.matmul(bank[h % 2][:, 0:NTOK], w_uv[:, r, h * P:(h + 1) * P], qlT[:, r, h, :], start=(r == 0), stop=(r == 1))
                mm.then_inc(om_mm, 1)
                if h:
                    value_sum(h - 1)
            value_sum(MH - 1)

            def product(g, m, x_hi, x_lo, ready):
                s, b = (OUT0 + m // 2) % RING, bank[m % 4][:, 0:NTOK]
                wait(pe, w_split, g + 1)
                for k in range(KT):
                    if m == 0:
                        wait(pe, *ready(k))
                    hi, lo = w_hi[:, m % 2, k, :], slab_lo[s][:, k, (m % 2) * P:(m % 2 + 1) * P]
                    pe.matmul(b, hi, x_hi[:, k, :], start=(k == 0), stop=False)
                    pe.matmul(b, hi, x_lo[:, k, :], start=False, stop=False)
                    mm = pe.matmul(b, lo, x_hi[:, k, :], start=False, stop=(k == KT - 1))
                mm.then_inc(tile_mm, 1)
            for n in range(KT):
                if n >= 4:
                    pe.wait_ge(x_added, n - 3)
                product(n, n, o_hi, hT_lo, lambda k: (h_split, k + 1))

            def ln_sums(r):
                pe.wait_ge(x_acc1, KT * (r + 1))
                pe.matmul(bank[4][:, 0:NTOK], ones, lnb[:, 0, :], start=True, stop=True)
                pe.wait_ge(x_acc2, KT * (r + 1))
                pe.matmul(bank[5][:, 0:NTOK], ones, lnb[:, 1, :], start=True, stop=True).then_inc(ln_mm, 1)
            ln_sums(0)
            with pe.Fori(0, 4) as q:
                for m in range(KT):
                    wait(pe, *((x_added, q * KT + (KT + m - 3)) if m < 4 else (up_relu, q * KT + (m - 3))))
                    product(q * 2 * KT + (KT + m), m, x_hi, hT_lo, lambda k: (h_split, KT + k + 1))
                for m in range(KT):
                    wait(pe, *((up_relu, q * KT + (KT + m - 3)) if m < 4 else (x_added, q * KT + (KT + m - 3))))
                    product(q * 2 * KT + (2 * KT + m), m, f_hi, f_lo, lambda k: (f_split, q * KT + (k + 1)))
            ln_sums(1)
            for n in range(12):
                g, q = n // 3, n % 3
                w = P if q < 2 else 32
                pe.wait_ge(ln_x, KT + 4 * g + 4)
                if n >= 4:
                    pe.wait_ge(y_rows_a if n % 2 else y_rows_d, (n - 4) // 2 + 1)
                for e in range(4):
                    tr = pe.transpose(bank[n % 4][0:w, e * P:(e + 1) * P], xT[:, 4 * g + e, q * P:q * P + w], ident)
                tr.then_inc(y_T, 1)
        @block.vector
        def _(dve):
            ch = Chain(dve, dve_step)
            dve.wait_ge(c_sig, 1)
            dve.tensor_tensor(crow[0:9, 2, :], crow[0:9, 0, :], crow[0:9, 1, :], ALU.mult).then_inc(c_silu, 1)
            dve.wait_ge(c_turned, 1)
            dve.wait_ge(padded, 3)
            dve.tensor_copy(cT[:, 0:9 * KT], bank[0][:, 0:9 * KT]).then_inc(c_ready, 1)
            dve.wait_ge(sh_turned, 1)
            cols = bank[2][:, 0:28 * NS].rearrange("p (k n) -> p k n", k=28)
            dve.tensor_copy(shT[:, 0:24, :], cols[:, 0:24, :])
            dve.tensor_copy(shT[0:LORA, 24:26, :], cols[0:LORA, 24:26, :])
            dve.tensor_copy(shT[:, 26:28, :], cols[:, 26:28, :]).then_inc(sh_ready, 1)
            for k in range(KT):
                dve.wait_ge(x_turned, k + 1)
                dve.tensor_copy(xT[:, k, :], bank[4 + k % 4][:, 0:NTOK]).then_inc(x_ready, 1)

            dve.wait_ge(par_ready, 1)

            def mod_add(i, u, col=0):
                dve.wait_ge(ada_sum, i * RING + (u + 1))
                t = i * 2 * RING + 2 * u
                dve.tensor_tensor(mod[:, bass.ds(t, 2), :],
                                  bank[4 + u % 2][:, col:col + 18].rearrange("p (k n) -> p k n", k=2),
                                  par[:, bass.ds(t, 2)].rearrange("p (k o) -> p k o", o=1).to_broadcast([P, 2, 9]),
                                  ALU.add).then_inc(mod_ready, 1)
            with dve.Fori(0, N_ADA // RING) as i:
                for u in range(RING):
                    mod_add(i, u)
            dve.wait_ge(mod_ready, N_ADA)
            ch.link(dve.tensor_scalar(mod[:, 16:32, :], mod[:, 16:32, :], 1.0, None, ALU.add))
            for k in range(KT):
                tok = lambda v: v[:, k, NP_TOK:NTOK].rearrange("p (s t) -> p s t", t=TS)
                per = lambda s: mod[:, s + k, 1:9].rearrange("p (s o) -> p s o", o=1).to_broadcast([P, NS, TS])
                ch.link(dve.tensor_tensor(tok(hT), tok(xT), per(16), ALU.mult))
                dve.tensor_tensor(tok(hT), tok(hT), per(0), ALU.add)
                dve.tensor_scalar(hT[:, k, 0:NP_TOK], xT[:, k, 0:NP_TOK], mod[:, 16 + k, 0:1], mod[:, k, 0:1],
                                  ALU.mult, ALU.add).then_inc(h_ready, 1)

            def shift_tile(mt, par_, out, mu, w, ch):
                dve.wait_ge(win_copied, mt + 1)
                src, d = pad[0:w, par_, :], dif[0:w, par_, :]
                ch.link(dve.tensor_tensor(d, src[:, 0:296], src[:, 1:297], ALU.subtract))
                dve.scalar_tensor_tensor(out[:, :, 0:NP_TOK].rearrange("p o n -> p (o n)"), d[:, 0:NP_TOK], mu,
                                         src[:, 1:1 + NP_TOK], ALU.mult, ALU.add)
                dve.scalar_tensor_tensor(
                    out[:, :, NP_TOK:NTOK].rearrange("p o (s t) -> p (o s) t", t=TS),
                    d[:, 256:296].rearrange("p (s t) -> p s t", t=5)[:, :, 1:5], mu,
                    src[:, 257:297].rearrange("p (s t) -> p s t", t=5)[:, :, 1:5], ALU.mult, ALU.add).then_inc(z_ready, 1)
            for mt, w in enumerate((LORA, LORA, P, P)):
                shift_tile(mt, mt % 2, zl[0:w, mt:mt + 1, :], par[0:w, 262 + mt:263 + mt], w, ch)
            with dve.Fori(0, 3) as i:
                ch.enter(i, 8)
                for m in range(8):
                    shift_tile(i * 8 + (4 + m), m % 2, z[:, bass.ds(i * 8 + m, 1), :], par[:, bass.ds(i * 8 + (96 + m), 1)], P, ch)
            ch.leave(3)
            for c in range(7):
                dve.wait_ge(last_turned, c + 1)
                if c == 6:
                    b = bank[c % 4]
                    dve.tensor_copy(last_rows[0:9, 0, 24 * P:24 * P + LORA], b[0:9, 0:LORA])
                    dve.tensor_copy(last_rows[0:9, 0, 24 * P + LORA:24 * P + 2 * LORA], b[0:9, P:P + LORA])
                    dve.tensor_copy(last_rows[0:9, 0, 24 * P + 2 * LORA:N_SHIFT], b[0:9, 2 * P:4 * P]).then_inc(last_out, 1)
                else:
                    dve.tensor_copy(last_rows[0:9, 0, c * 512:(c + 1) * 512], bank[c % 4][0:9, :]).then_inc(last_out, 1)
            for j in range(RT):
                dve.wait_ge(lora_mm, 2 * j + 2)
                dve.tensor_copy(hT[:, 8 + j, :], bank[4 + j % 2][:, 0:NTOK]).then_inc(g_ready, 1)
            for j in range(RT):
                n = nrm[:, j % 2, :]
                dve.wait_ge(kk_nrm, j + 1)
                ch.link(dve.tensor_scalar(n, n, 1e-12, None, ALU.max))
                ch.link(dve.reciprocal(n, n))
                dve.wait_ge(kk_raw, j + 1)
                dve.tensor_tensor(hT[:, j, :], hT[:, j, :], n, ALU.mult).then_inc(kk_ready, 1)

            def tile_of(v, j):
                return v[:, bass.ds(j, 1), :].rearrange("p o n -> p (o n)")

            def bcast(v, n):
                return v.rearrange("p (o t) -> p o t", o=1).to_broadcast([v.shape[0], n, v.shape[1]])

            def scan(j):
                dve.wait_ge(lora_sig, 2 * RT)
                if not first(j):
                    dve.wait_ge(ew_kv, j)
                dve.tensor_scalar(kmul, tile_of(ag, j), par[:, bass.ds(j + 152, 1)], omka[:, bass.ds(j, 1)], ALU.mult, ALU.add)
                if not first(j):
                    dve.wait_ge(ew_exp, j)
                dve.tensor_tensor_scan(lam, const[:, C_SCAN:C_SCAN + NTOK], tile_of(sigw, j), 0.0, ALU.mult, ALU.add).then_inc(ew_scan, 1)

            def elementwise(j, u):
                abr, bk, rv, pend = ew_buf[u]
                dve.wait_ge(ew_exp, j + 1)
                if not (isinstance(j, int) and j < 2):
                    dve.wait_ge(pe_tile, j * PE_N + (PE_O - 2 * PE_N))
                ch.link(dve.scalar_tensor_tensor(abr[:, 0, :], tile_of(hT, j), -1.0, dec[:, 2, :], ALU.mult, ALU.mult))
                dve.wait_ge(ew_pool, j + 1)
                dve.tensor_copy(arS[u][:, 0:32], abr[:, 0, NP_TOK:NTOK])
                dve.tensor_copy(arS[u][:, 32:64], abr[:, 2, NP_TOK:NTOK]).then_inc(ew_a, 1)
                if not first(j):
                    dve.wait_ge(pe_tile, j * PE_N + (PE_BON - PE_N))
                dve.wait_ge(ew_kv, j + 1)
                dve.scalar_tensor_tensor(rkk, tile_of(z, j), par[:, bass.ds(j + 160, 1)], tile_of(z, j + 8), ALU.mult, ALU.mult).then_inc(ew_rk, 1)

            def tile(j, u, ahead=True):
                abr, bk, rv, pend = ew_buf[u]
                four = lambda b: bank[b][:, :].rearrange("p (c t) -> p c t", c=4)
                dve.wait_ge(act_tile, j * ACT_N + ACT_A4)
                two = lambda v: v.rearrange("p (h q) t -> p h q t", h=2)
                a4_h = a4.rearrange("p (h w q) t -> p h w q t", h=2, w=2)
                both = lambda c0: const[:, c0:c0 + P].rearrange("p (a b t) -> p a b t", a=1, b=1).to_broadcast([P, 2, 2, P])
                ch.mark(dve.tensor_tensor(two(tm), a4_h[:, :, 0], both(C_M2), ALU.mult))
                ch.link(dve.tensor_tensor(two(tt), a4_h[:, :, 1], both(C_M2T), ALU.mult))
                dve.tensor_tensor(tm, tm, bcast(ident, 4), ALU.add)
                dve.tensor_tensor(tt, tt, bcast(ident, 4), ALU.add).then_inc(e_t, 1)
                dve.wait_ge(pe_tile, j * PE_N + PE_RV)
                dve.tensor_copy(uv[64:128], bank[1][64:128, :].rearrange("p (c t) -> p c t", c=4)).then_inc(dve_tile, 1)
                dve.wait_ge(act_tile, j * ACT_N + ACT_SMP)
                dve.tensor_copy(uvs[32:64, :], bank[7][32:64, P:2 * P])
                for h in range(2):
                    ch.mark(dve.tensor_tensor(ars[0:64, h, :], bank[7 - h][0:64, 256:320], const[0:64, C_ARS:C_ARS + 64], ALU.mult))
                    ch.mark(dve.tensor_tensor(ts_m[0:32, h, :], bank[7 - h][0:32, 320:352], const[0:32, C_M2:C_M2 + 32], ALU.mult))
                ch.wait()
                ch.mark(dve.tensor_tensor(ts_m[0:32], ts_m[0:32], bcast(const[0:32, C_ID:C_ID + 32], 2), ALU.add))
                ch.mark(dve.tensor_tensor(ts_t[0:32], ars[0:32, :, 0:32], bcast(const[0:32, C_M2T:C_M2T + 32], 2), ALU.mult))
                ch.wait()
                dve.tensor_tensor(ts_t[0:32], ts_t[0:32], bcast(const[0:32, C_ID:C_ID + 32], 2), ALU.add)
                dve.tensor_tensor(ts_n[0:32], ars[0:32, :, 0:32], bcast(const[0:32, C_LVL:C_LVL + 32], 2), ALU.mult).then_inc(dve_tile, 1)
                dve.wait_ge(pe_tile, j * PE_N + PE_AR)
                for h in range(2):
                    ins = dve.tensor_tensor(ar[:, h * NCH:(h + 1) * NCH, :], four(2 + h), bcast(const[:, C_AR:C_AR + P], 4), ALU.mult)
                ins.then_inc(dve_tile, 1)
                if ahead:
                    scan(j + 1)

                def between(n):
                    if n == 0:
                        dve.wait_ge(pe_tile, j * PE_N + PE_BON)
                        v = tile_of(z, j + 16)
                        dve.tensor_tensor(v, bank[1][:, 0:NTOK], v, ALU.mult).then_inc(dve_tile, 1)
                    if n == 1:
                        dve.wait_ge(pe_tile, j * PE_N + PE_DS)
                        if not first(j):
                            dve.wait_ge(pe_tile, j * PE_N + (PE_SN - PE_N))
                        for h in range(2):
                            ch.link(dve.tensor_tensor(
                                uve[0:64, h, :].rearrange("p (s v) -> p s v", s=NS),
                                bank[2 + h][0:64, :].rearrange("p (s v) -> p s v", s=NS),
                                const[0:64, C_SEQ:C_SEQ + NS].rearrange("p (s o) -> p s o", o=1).to_broadcast([64, NS, 64]), ALU.mult))
                            ins = dve.tensor_reduce(ds[0:64, h, :], uve[0:64, h, :].rearrange("p (s v) -> p v s", s=NS), AX.X, ALU.add)
                            ins.then_inc(dve_tile, 1) if h else ch.mark(ins)
                    if n == 2:
                        dve.wait_ge(pe_tile, j * PE_N + PE_TS)
                        dve.tensor_tensor(ts_t[0:32], ts_t[0:32], bank[7][0:32, 64:128].rearrange("p (h c) -> p h c", h=2), ALU.add).then_inc(dve_tile, 1)
                        dve.wait_ge(pe_tile, j * PE_N + PE_XS)
                        dve.wait_ge(dve_tile, j * DVE_N + DVE_DS)
                        dve.tensor_tensor(d_smp[0:32, :], bank[7][0:32, P:2 * P], ds[0:32].rearrange("p h v -> p (h v)"), ALU.add).then_inc(dve_tile, 1)
                    if n == 4:
                        dve.wait_ge(pe_tile, j * PE_N + PE_OS)
                        dve.tensor_tensor(o_smp[32:64, :], bank[7][32:64, 384:512], ds[32:64].rearrange("p h v -> p (h v)"), ALU.add).then_inc(dve_tile, 1)
                for n in range(5):
                    between(n)
                    dve.wait_ge(p_inc, j * 5 + (n + 1))
                    dve.wait_ge(e_t, j * 6 + (n + 1))
                    if n < 4:
                        dve.tensor_tensor(tm, tm, four(4), ALU.add)
                    dve.tensor_tensor(tt, tt, four(5), ALU.add).then_inc(e_t, 1)
                if ahead:
                    elementwise(j + 1, 1 - u)
                for c in range(NCH):
                    dve.wait_ge(p_u, j * NCH + (c + 1))
                    dve.tensor_copy(uv[0:64, c, :], bank[7][0:64, 0:P]).then_inc(e_u, 1)
                    if c:
                        dve.wait_ge(e_st, j * NCH + c)
                        ch.mark(dve.tensor_scalar(st_dec, st[:, (c - 1) % 2, :], pend[:, c:c + 1], None, ALU.mult))
                    dve.wait_ge(p_s, j * NCH + (c + 1))
                    if c:
                        ch.wait()
                        dve.scalar_tensor_tensor(st[:, c % 2, :], bank[2][:, 0:HD], pend[:, c:c + 1], st_dec, ALU.mult, ALU.add).then_inc(e_st, 1)
                    else:
                        dve.tensor_scalar(st[:, 0, :], bank[2][:, 0:HD], pend[:, 0:1], None, ALU.mult).then_inc(e_st, 1)
                    if c == 0:
                        dve.wait_ge(pe_tile, j * PE_N + PE_SN)
                        flat = s0t.rearrange("p q n -> p (q n)")
                        ch.link(dve.tensor_tensor(flat, bank[6][:, :], flat, ALU.add))
                        by_seq = flat.rearrange("p (s v) -> p s v", s=NS)
                        dve.tensor_tensor(by_seq, by_seq, pend[:, NCH:NCH + NS].rearrange("p (s o) -> p s o", o=1).to_broadcast([P, NS, 64]),
                                          ALU.mult).then_inc(dve_tile, 1)
                    mod_add(j, N_ADA + c, 256)
            ch.link(dve.tensor_scalar(omka, par[:, 128 + 24:128 + 32], -1.0, 1.0, ALU.mult, ALU.add))
            scan(0)
            elementwise(0, 0)
            tile(0, 0)
            tile(1, 1)
            with dve.Fori(1, RT // 2 - 1) as i:
                ch.enter(i - 1, 2 * TILE_MARKS)
                for u in range(2):
                    tile(i * 2 + u, u)
            ch.leave(RT // 2 - 2)
            tile(RT - 2, 0)
            tile(RT - 1, 1, False)
            dve.wait_ge(mod_ready, N_ADA + N_LATE)
            ch.mark(dve.tensor_scalar(mod[:, 64:80, :], mod[:, 64:80, :], 1.0, None, ALU.add))
            for j in range(RT):
                mean, var = nrm[:, j % 2, :], gnv[:, j % 2, :]
                dve.wait_ge(gn_mm, j + 1)
                if j >= 2:
                    dve.wait_ge(gn_cen, j - 1)
                ch.link(dve.tensor_scalar(mean, bank[j % 2][:, 0:NTOK], 1.0 / HD, None, ALU.mult))
                ch.link(dve.tensor_tensor(dif288, mean, mean, ALU.mult))
                dve.scalar_tensor_tensor(var, bank[2 + j % 2][:, 0:NTOK], 1.0 / HD, dif288, ALU.mult, ALU.subtract).then_inc(gn_var, 1)
                dve.wait_ge(gn_std, j + 1)
                ch.link(dve.reciprocal(var, var))
                dve.wait_ge(gn_cen, j + 1)
                ch.link(dve.tensor_tensor(hT[:, j, :], hT[:, j, :], var, ALU.mult))
                dve.tensor_scalar(hT[:, j, :], hT[:, j, :], par[:, P + 40 + j:P + 41 + j], par[:, P + 48 + j:P + 49 + j],
                                  ALU.mult, ALU.add).then_inc(gn_nrm, 1)
            cos, sin = const[0:64, C_COS:C_COS + NTOK], const[0:64, C_SIN:C_SIN + NTOK]
            for n in range(2):
                dve.wait_ge(m_std, n + 1)
                ch.link(dve.reciprocal(rin[:, n, :], rin[:, n, :]))
                for k in range(4 if n == 0 else 2):
                    dst = cqn[:, k, :] if n == 0 else latT[:, k, :]
                    g = 256 + 4 * n + k
                    dve.scalar_tensor_tensor(dst, mla[:, 4 * n + k, :], par[:, g:g + 1], rin[:, n, :], ALU.mult, ALU.mult).then_inc(m_ready, 1)

            def rotate(dst, raw, turned, done):
                ch.mark(dve.tensor_tensor(rot_a[0:64], raw, cos, ALU.mult))
                ch.link(dve.tensor_tensor(rot_b[0:64], turned, sin, ALU.mult))
                dve.tensor_tensor(dst, rot_a[0:64], rot_b[0:64], ALU.add).then_inc(done, 1)
            dve.wait_ge(m_mm, 3)
            rotate(krT[0:64, :], mla[0:64, 6, :], bank[6][0:64, 0:NTOK], kr_ready)
            for h in range(MH):
                dve.wait_ge(q_rot, h + 1)
                if h == 0:
                    dve.wait_ge(kr_ready, 1)
                else:
                    dve.wait_ge(qr_ready, h)
                rotate(qrT[0:64, h, :], qraw[0:64, h % 2, :], bank[4 + h % 2][0:64, 0:NTOK], qr_ready)
            for n in range(2 * MH):
                h, q = n // 2, n % 2
                nk, Sn = (q + 1) * P, S2[:, q, :]
                mx, total = sm[:, q:q + 1], sm[:, 2 + q:3 + q]
                dve.wait_ge(pa_s, n + 1)
                if n >= 2:
                    dve.wait_ge(pa_T, n - 1)
                if q:
                    ch.mark(dve.tensor_copy(Sn[:, 0:P], bank[4 + q][:, 0:P]))
                ch.link(dve.tensor_tensor(Sn[:, nk - P:nk], bank[4 + q][:, nk - P:nk], const[:, C_CAUS:C_CAUS + P], ALU.add))
                ch.link(dve.tensor_reduce(mx, Sn[:, 0:nk], AX.X, ALU.max))
                dve.tensor_scalar(mx, mx, -SM_SCALE, None, ALU.mult).then_inc(pa_max, 1)
                dve.wait_ge(pa_exp, n + 1)
                ch.link(dve.reciprocal(total, total))
                dve.tensor_scalar(Sn[:, 0:nk], Sn[:, 0:nk], total, None, ALU.mult).then_inc(pa_p, 1)
                dve.wait_ge(pa_ctx, n + 1)
                dve.tensor_copy(qlT[:, :, h, q * P:(q + 1) * P], bank[7][:, 0:256].rearrange("p (r n) -> p r n", r=2)).then_inc(pa_ready, 1)
            for g in range(2):
                def copy_scores(kb):
                    dve.wait_ge(sa_s, g * 9 + kb + 1)
                    if kb < 8:
                        dve.tensor_copy(S[:, kb * 256:(kb + 1) * 256], bank[5 + kb % 2][:, 0:256]).then_inc(sa_copied, 1)
                    else:
                        dve.tensor_tensor(S[:, 2048:2080], bank[5][:, 0:32], const[:, C_NEW + 32 * g:C_NEW + 32 * g + 32], ALU.add).then_inc(sa_copied, 1)
                for kb in range(8):
                    m = g * 8 + kb
                    dve.wait_ge(sa_tr, m * 4 + 2)
                    if kb or g:
                        dve.wait_ge(sa_s, g * 9 + kb)
                    dve.tensor_copy(krS[0:64, 0, :], bank[4][0:64, :]).then_inc(sa_kr, 1)
                    dve.wait_ge(sa_tr, m * 4 + 4)
                    dve.tensor_copy(krS[0:64, 1, :], bank[7][0:64, :]).then_inc(sa_kr, 1)
                    dve.tensor_copy(latS[:, 3, :], bank[3][:, :]).then_inc(sa_kr, 1)
                    if kb:
                        copy_scores(kb - 1)
                copy_scores(7)
                copy_scores(8)
                dve.wait_ge(sa_copied, g * 9 + 9)
                ch.link(dve.tensor_reduce(sm[:, 4:5], S, AX.X, ALU.max))
                dve.tensor_scalar(sm[:, 4:5], sm[:, 4:5], -SM_SCALE, None, ALU.mult).then_inc(sa_max, 1)
                for b in (1, 3):
                    dve.wait_ge(sa_T, g * 5 + b + 1)
                    dve.tensor_copy(pT[:, 4 * b:4 * b + 4, :], bank[b][:, :].rearrange("p (k q) -> p k q", k=4)).then_inc(sa_kr, 1)
                dve.wait_ge(sa_exp, g + 1)
                dve.reciprocal(sm[:, 6:7], sm[:, 5:6]).then_inc(sa_rinv, 1)
                dve.wait_ge(sa_ctxT, g + 1)
                for r in range(2):
                    ins = dve.tensor_copy(qlT[:, r, :, NP_TOK + 16 * g:NP_TOK + 16 * g + 16].rearrange("p h (s t) -> p h s t", t=TS),
                                          bank[7][:, r * P:(r + 1) * P].rearrange("p (s h t) -> p h s t", s=4, h=MH))
                ins.then_inc(sa_ready, 1)
            def split_weights(g, m):
                s, c = (OUT0 + m // 2) % RING, slice((m % 2) * P, (m % 2 + 1) * P)
                if m % 2 == 0:
                    dve.wait_ge(slab_in[s], (g - m) * 2 + slab_ready(OUT0 + m // 2))
                if not (isinstance(g, int) and g < 2):
                    dve.wait_ge(tile_mm, g - 1)
                ch.link(dve.tensor_copy(w_hi[:, m % 2], slab[s][:, :, c]))
                dve.tensor_tensor(slab_lo[s][:, :, c], slab[s][:, :, c], w_hi[:, m % 2].bitcast(F32), ALU.subtract).then_inc(w_split, 1)

            def split_rows(hi, lo, v, done):
                ch.link(dve.tensor_copy(hi, v))
                dve.tensor_tensor(lo, v, hi.bitcast(F32), ALU.subtract).then_inc(done, 1)
            split_weights(0, 0)
            split_weights(1, 1)
            dve.wait_ge(gn_ready, RT)
            for k in range(RT):
                split_rows(o_hi[:, k, :], hT_lo[:, k, :], hT[:, k, :], h_split)
            rs = lnb[:, 3, :]
            dve.wait_ge(om_std, 1)
            ch.link(dve.reciprocal(rs, rs))
            for h in range(MH):
                ch.mark(dve.scalar_tensor_tensor(hT[:, 8 + h, :], hT[:, 8 + h, :], par[:, P + 56 + h:P + 57 + h], rs, ALU.mult, ALU.mult))
            ch.wait()
            for h in range(MH):
                split_rows(o_hi[:, 8 + h, :], hT_lo[:, 8 + h, :], hT[:, 8 + h, :], h_split)

            def by_sequence(v):
                return v.rearrange("p (s t) -> p s t", t=TS)

            def gate(k, section):
                return mod[:, section + k, 1:9].rearrange("p (s o) -> p s o", o=1).to_broadcast([P, NS, TS])

            def add_gated(n, section, mm_value, xa):
                b = bank[n % 4]
                dve.wait_ge(tile_mm, mm_value)
                dve.wait_ge(xa, n + 1)
                tmp = lnb[:, 6 + n % 2, 0:32]
                ch.link(dve.tensor_tensor(by_sequence(tmp), by_sequence(b[:, NP_TOK:NTOK]), gate(n, section), ALU.mult))
                dve.tensor_tensor(xT[:, n, NP_TOK:NTOK], xT[:, n, NP_TOK:NTOK], tmp, ALU.add)
                dve.scalar_tensor_tensor(xT[:, n, 0:NP_TOK], b[:, 0:NP_TOK], mod[:, section + n, 0:1], xT[:, n, 0:NP_TOK],
                                         ALU.mult, ALU.add).then_inc(x_added, 1)

            def add_square(r, n):
                dve.wait_ge(x_sq, r * KT + n + 1)
                if n == 0:
                    dve.tensor_copy(lnb[:, 1, :], lnb[:, 4, :]).then_inc(x_acc2, 1)
                else:
                    dve.wait_ge(x_acc2, r * KT + n)
                    dve.tensor_tensor(lnb[:, 1, :], lnb[:, 1, :], lnb[:, 4 + n % 2, :], ALU.add).then_inc(x_acc2, 1)
            for n in range(KT):
                split_weights(n + 2, (n + 2) % 8)
                add_gated(n, 32, n + 1, xa_ready)
                if n:
                    add_square(0, n - 1)
            add_square(0, KT - 1)

            def norm(r):
                mean, rstd = lnb[:, 2, :], lnb[:, 3, :]
                dve.wait_ge(ln_mm, r + 1)
                ch.link(dve.tensor_scalar(mean, bank[4][:, 0:NTOK], 1.0 / D, None, ALU.mult))
                ch.link(dve.tensor_tensor(lnb[:, 6, :], mean, mean, ALU.mult))
                dve.scalar_tensor_tensor(rstd, bank[5][:, 0:NTOK], 1.0 / D, lnb[:, 6, :], ALU.mult, ALU.subtract).then_inc(ln_var, 1)
                dve.wait_ge(ln_std, r + 1)
                dve.reciprocal(rstd, rstd).then_inc(ln_rstd, 1)
                dve.wait_ge(ln_rstd, r + 1)

            def scale_tile(r, k):
                dve.wait_ge(ln_cen, r * KT + k + 1)
                dve.tensor_tensor(xT[:, k, :], xT[:, k, :], lnb[:, 3, :], ALU.mult).then_inc(ln_nrm, 1)

            def modulate(k):
                dve.wait_ge(ln_x, k + 1)
                smp_ = hT[:, k, NP_TOK:NTOK]
                ch.link(dve.tensor_tensor(by_sequence(smp_), by_sequence(xT[:, k, NP_TOK:NTOK]), gate(k, 64), ALU.mult))
                dve.tensor_tensor(by_sequence(smp_), by_sequence(smp_), gate(k, 48), ALU.add)
                dve.tensor_scalar(hT[:, k, 0:NP_TOK], xT[:, k, 0:NP_TOK], mod[:, 64 + k, 0:1], mod[:, 48 + k, 0:1],
                                  ALU.mult, ALU.add).then_inc(h2_ready, 1)
                dve.wait_ge(h2_ready, k + 1)
                split_rows(x_hi[:, k, :], hT_lo[:, k, :], hT[:, k, :], h_split)
            norm(0)
            dve.wait_ge(tile_mm, KT)
            for k in range(KT):
                scale_tile(0, k)
                if k:
                    modulate(k - 1)
            modulate(KT - 1)
            def quarter(q, last):
                for m in range(2 * KT):
                    if not (last and m >= 2 * KT - 2):
                        split_weights(q * 2 * KT + (KT + m + 2), (m + 2) % 8)
                    if m < KT:
                        dve.wait_ge(up_f, q * KT + (m + 1))
                        split_rows(f_hi[:, m, :], f_lo[:, m, :], relu_sq[:, m % 2, :], f_split)
                    else:
                        add_gated(m - KT, 80, q * 2 * KT + (KT + m + 1), xa2_ready)
                        if last and m > KT:
                            add_square(1, m - KT - 1)
            with dve.Fori(0, 3) as q:
                ch.enter(q, 4 * KT)
                quarter(q, False)
            ch.leave(3)
            quarter(3, True)
            add_square(1, KT - 1)
            norm(1)
            for k in range(KT):
                scale_tile(1, k)
            for n in range(0, 12, 2):
                q = n % 3
                rows = P if q < 2 else 32
                dve.wait_ge(y_T, n + 1)
                dve.tensor_copy(y_rows[0:rows, q, (n // 3) * 512:(n // 3 + 1) * 512], bank[n % 4][0:rows, :]).then_inc(y_rows_d, 1)


OUTS = {
    "y_prompt": (1, NP_TOK, D), "y_sample": (NS, TS, D),
    "new_latent_prompt": (1, 1, NP_TOK, KVR), "new_krope_prompt": (1, 1, NP_TOK, ROPE),
    "new_wkv_prompt": (1, 1, 2 * RT, HD, HD), "new_shift_prompt": (1, 1, N_SHIFT),
    "new_latent_sample": (1, NS, TS, KVR), "new_krope_sample": (1, NS, TS, ROPE),
    "new_wkv_sample": (1, NS, 2 * RT, HD, HD), "new_shift_sample": (1, NS, N_SHIFT),
}


def kernel(**inputs):
    import numpy as _np
    import concourse.bacc as _bacc
    from concourse.bass_utils import run_bass_kernel_spmd as _run

    nc = _bacc.Bacc("TRN2", target_bir_lowering=False, num_devices=1)
    arrays, aps = {}, {}
    for name, value in list(inputs.items()) + [("const", shape_constants())]:
        v = _np.ascontiguousarray(value)
        arrays[f"in_{name}_dram"] = v
        aps[name] = nc.dram_tensor(f"in_{name}_dram", v.shape, mybir.dt.from_np(v.dtype), kind="ExternalInput").ap()
    for name, shape in OUTS.items():
        aps[name] = nc.dram_tensor(f"out_{name}_dram", shape, F32, kind="ExternalOutput").ap()
    build(nc, aps)
    r = _run(nc, [arrays], core_ids=[0])
    return tuple(r.results[0][f"out_{name}_dram"] for name in OUTS)
```
